# Optimizing a Trainium2 kernel written in Bass

```python
import jax, jax.numpy as jnp
from jax import lax
import numpy as np

D_MODEL = 1024
BATCH = 1
SEQ = 1024
DEPTH = 1

HEAD_DIM = 64
DILATED_GROUPS = ((128, 1), (512, 4), (2048, 16))
N_GROUPS = 3
HEADS_PER_GROUP = 8
ATTN_HEADS = N_GROUPS * HEADS_PER_GROUP
ATTN_QKV_WIDTH = ATTN_HEADS * HEAD_DIM
ATTN_WIDTH = HEADS_PER_GROUP * HEAD_DIM
CONV_WIDTH = D_MODEL // 2
CONV_KERNEL = 31
N_BRANCHES = 2
NORM_EPS = 1e-6
SPLITS = (ATTN_QKV_WIDTH, ATTN_QKV_WIDTH, ATTN_QKV_WIDTH, ATTN_WIDTH, 2 * CONV_WIDTH, CONV_WIDTH, N_BRANCHES * D_MODEL)
IN_WIDTH = 1536 * 3 + 512 + 1024 + 512 + 2048

kernel_name = "hybrid_dilated_attn_conformer_gated_merge"

def rms_norm(x, w):
    xf = x.astype(jnp.float32)
    y = xf * lax.rsqrt(jnp.mean(xf * xf, axis=-1, keepdims=True) + NORM_EPS)
    return (y * w.astype(jnp.float32)).astype(x.dtype)

def layer_norm(x, w, b):
    xf = x.astype(jnp.float32)
    mu = jnp.mean(xf, axis=-1, keepdims=True)
    var = jnp.mean(jnp.square(xf - mu), axis=-1, keepdims=True)
    y = (xf - mu) * lax.rsqrt(var + NORM_EPS)
    return (y * w.astype(jnp.float32) + b.astype(jnp.float32)).astype(x.dtype)

def dilated_window_attention(q, k, v, window, dilation):
    B, S, H, Dh = q.shape
    d = dilation
    n = window // dilation
    L = S // d
    nb = -(-L // n)
    Lp = nb * n

    def to_sub(t):
        t = t.reshape(B, L, d, H, Dh).transpose(0, 2, 1, 3, 4).reshape(B * d, L, H, Dh)
        return jnp.pad(t, ((0, 0), (0, Lp - L), (0, 0), (0, 0)))

    qs, ks, vs = to_sub(q), to_sub(k), to_sub(v)
    BD = B * d
    qb = qs.reshape(BD, nb, n, H, Dh)

    def band(t):
        tp = jnp.pad(t, ((0, 0), (n, 0), (0, 0), (0, 0))).reshape(BD, nb + 1, n, H, Dh)
        return jnp.concatenate([tp[:, :-1], tp[:, 1:]], axis=2)

    kb, vb = band(ks), band(vs)
    s = jnp.einsum('bnqhd,bnkhd->bnhqk', qb, kb).astype(jnp.float32)
    blk = jnp.arange(nb)[:, None, None]
    qi = jnp.arange(n)[None, :, None]
    kj = jnp.arange(2 * n)[None, None, :]
    dist = qi + n - kj
    valid = (dist >= 0) & (dist <= n) & (blk * n - n + kj >= 0)
    s = jnp.where(valid[None, :, None], s, -jnp.inf)
    m = jnp.max(s, axis=-1, keepdims=True)
    p = jnp.exp(s - m)
    denom = jnp.sum(p, axis=-1, keepdims=True)
    o = jnp.einsum('bnhqk,bnkhd->bnqhd', p, vb.astype(jnp.float32))
    o = o / denom.transpose(0, 1, 3, 2, 4)
    lse = (m + jnp.log(denom))[..., 0].transpose(0, 1, 3, 2)

    def from_sub(t):
        rest = t.shape[3:]
        t = t.reshape((B, d, Lp) + rest)[:, :, :L]
        t = jnp.moveaxis(t, 1, 2)
        return t.reshape((B, S) + rest)

    return from_sub(o), from_sub(lse)

def depthwise_causal_conv(u, w, b):
    C = u.shape[-1]
    y = lax.conv_general_dilated(u, w.astype(u.dtype)[:, None, :], window_strides=(1,),
                                 padding=((CONV_KERNEL - 1, 0),),
                                 dimension_numbers=('NWC', 'WIO', 'NWC'),
                                 feature_group_count=C)
    return y + b.astype(u.dtype)

def hybrid_layer(x, c, w_ada, b_ada, norm_w, w_in, b_gate, q_norm_w, k_norm_w,
                 w_attn_proj, conv_w, conv_b, conv_ln_w, conv_ln_b, w_conv_proj, w_out):
    B, S, D = x.shape
    ada = jax.nn.silu(c) @ w_ada + b_ada
    shift, scale, gate = jnp.split(ada, 3, axis=-1)
    h = rms_norm(x, norm_w) * (1 + scale[:, None, :]) + shift[:, None, :]

    proj = h @ w_in
    offsets = tuple(int(o) for o in np.cumsum(SPLITS)[:-1])
    q, k, v, z_attn, u_conv, z_conv, g = jnp.split(proj, offsets, axis=-1)

    q = rms_norm(q.reshape(B, S, N_GROUPS, HEADS_PER_GROUP, HEAD_DIM), q_norm_w) * (HEAD_DIM ** -0.5)
    k = rms_norm(k.reshape(B, S, N_GROUPS, HEADS_PER_GROUP, HEAD_DIM), k_norm_w)
    v = v.reshape(B, S, N_GROUPS, HEADS_PER_GROUP, HEAD_DIM)
    outs, lses = [], []
    for gi, (window, dilation) in enumerate(DILATED_GROUPS):
        o, lse = dilated_window_attention(q[:, :, gi], k[:, :, gi], v[:, :, gi], window, dilation)
        outs.append(o)
        lses.append(lse)
    o_all = jnp.stack(outs, axis=0)
    wts = jax.nn.softmax(jnp.stack(lses, axis=0), axis=0)
    attn = jnp.sum(wts[..., None] * o_all, axis=0).reshape(B, S, ATTN_WIDTH).astype(x.dtype)
    y_attn = (attn * jax.nn.silu(z_attn)) @ w_attn_proj

    a_half, b_half = jnp.split(u_conv, 2, axis=-1)
    glu = a_half * jax.nn.sigmoid(b_half)
    cv = depthwise_causal_conv(glu, conv_w, conv_b)
    cv = jax.nn.silu(layer_norm(cv, conv_ln_w, conv_ln_b))
    y_conv = (cv * jax.nn.silu(z_conv)) @ w_conv_proj

    g_attn, g_conv = jnp.split(g + b_gate, 2, axis=-1)
    merged = jax.nn.sigmoid(g_attn) * y_attn + jax.nn.sigmoid(g_conv) * y_conv
    return x + gate[:, None, :] * (merged @ w_out)

def setup_inputs(seed: int = 0) -> dict:
    key = jax.random.key(seed)
    ks = jax.random.split(key, 18)
    f32 = jnp.float32

    def nrm(k, shape, scale):
        return jax.random.normal(k, shape, f32) * scale

    return {
        "x": nrm(ks[0], (BATCH, SEQ, D_MODEL), 1.0),
        "c": nrm(ks[1], (BATCH, D_MODEL), 1.0),
        "w_ada": nrm(ks[2], (DEPTH, D_MODEL, 3 * D_MODEL), D_MODEL ** -0.5),
        "b_ada": nrm(ks[3], (DEPTH, 3 * D_MODEL), 0.02),
        "norm_w": 1.0 + nrm(ks[4], (DEPTH, D_MODEL), 0.02),
        "w_in": nrm(ks[5], (DEPTH, D_MODEL, IN_WIDTH), D_MODEL ** -0.5),
        "b_gate": nrm(ks[6], (DEPTH, N_BRANCHES * D_MODEL), 0.02),
        "q_norm_w": 1.0 + nrm(ks[7], (DEPTH, HEAD_DIM), 0.02),
        "k_norm_w": 1.0 + nrm(ks[8], (DEPTH, HEAD_DIM), 0.02),
        "w_attn_proj": nrm(ks[9], (DEPTH, ATTN_WIDTH, D_MODEL), ATTN_WIDTH ** -0.5),
        "conv_w": nrm(ks[10], (DEPTH, CONV_KERNEL, CONV_WIDTH), CONV_KERNEL ** -0.5),
        "conv_b": nrm(ks[11], (DEPTH, CONV_WIDTH), 0.02),
        "conv_ln_w": 1.0 + nrm(ks[12], (DEPTH, CONV_WIDTH), 0.02),
        "conv_ln_b": nrm(ks[13], (DEPTH, CONV_WIDTH), 0.02),
        "w_conv_proj": nrm(ks[14], (DEPTH, CONV_WIDTH, D_MODEL), CONV_WIDTH ** -0.5),
        "w_out": nrm(ks[15], (DEPTH, D_MODEL, D_MODEL), D_MODEL ** -0.5),
    }

def reference(x, c, w_ada, b_ada, norm_w, w_in, b_gate, q_norm_w, k_norm_w,
              w_attn_proj, conv_w, conv_b, conv_ln_w, conv_ln_b, w_conv_proj, w_out):
    for l in range(DEPTH):
        x = hybrid_layer(x, c, w_ada[l], b_ada[l], norm_w[l], w_in[l], b_gate[l],
                         q_norm_w[l], k_norm_w[l], w_attn_proj[l], conv_w[l], conv_b[l],
                         conv_ln_w[l], conv_ln_b[l], w_conv_proj[l], w_out[l])
    return x


_drawn_inputs = setup_inputs


def setup_inputs(seed=0):
    import zlib

    import numpy as np

    out = dict(_drawn_inputs(seed))
    spreads = {}
    factors = {'b_ada': 5.369,
     'norm_w': 8.0,
     'b_gate': 22.643,
     'q_norm_w': 8.0,
     'k_norm_w': 8.0,
     'conv_b': 33.032,
     'conv_ln_w': 44.133,
     'conv_ln_b': 44.239}
    for name, (base, spread) in spreads.items():
        noise = np.random.default_rng([zlib.crc32(name.encode()), seed]).standard_normal(out[name].shape)
        drawn = base * np.exp(spread * noise) if base else spread * noise
        out[name] = __import__('jax').numpy.asarray(drawn.astype(out[name].dtype))
    for name, factor in factors.items():
        out[name] = (out[name] * factor).astype(out[name].dtype)
    return out
```

```python
from contextlib import ExitStack

import concourse.bass as bass
from concourse import mybir

P = 128
T = 1024
D = 1024
KB = D // P
NT = T // P
HALF = 512
CW = 512
CB = CW // P
TAPS = 31
PAD = TAPS - 1
HD = 64
PAIRS = 4
GROUPS = 3
DILATION = (1, 4, 16)
OW = 2 * HD + 4
EPS = 1e-6
MASKED = -1e30

Q0, K0, V0, ZA0, UA0, UB0, ZC0, GA0, GB0 = 0, 1536, 3072, 4608, 5120, 5632, 6144, 6656, 7680

F32 = mybir.dt.float32
F32R = mybir.dt.float32r
ALU = mybir.AluOpType
ACT = mybir.ActivationFunctionType

STAGES = PAIRS * GROUPS
SLOTS = 48


def blocks():
    out = []
    for c in range(CB):
        out += [("convb", c), ("conva", c), ("convz", c)]
    for i in range(KB // 2):
        out += [("gB", 2 * i), ("gB", 2 * i + 1), ("pB", i)]
    for st in range(STAGES):
        out += [("q", st), ("k", st), ("v", st)]
    out += [("gA", 0), ("gA", 1)] + [("z", p) for p in range(PAIRS)] + [("pA", 0)]
    for i in range(1, KB // 2):
        out += [("gA", 2 * i), ("gA", 2 * i + 1), ("pA", i)]
    out += [("out", k) for k in range(8)]
    return out


BLOCKS = blocks()
NO = {b: n for n, b in enumerate(BLOCKS)}


def segments():
    seg, last = {}, {}
    for n, (kind, w) in enumerate(BLOCKS):
        if kind == "out":
            continue
        parts = [(kind, w)] if kind not in ("pA", "pB") else [("y" + kind[1], 2 * w), ("y" + kind[1], 2 * w + 1)]
        for part in parts:
            for tt in range(2):
                last[n] = seg[(*part, tt)] = len(seg)
    return seg, last


SEG, LAST_SEG = segments()
RAW, WR = 2, 3


def build(nc, x, c, w_ada, b_ada, norm_w, w_in, b_gate, q_norm_w, k_norm_w, w_attn_proj,
          conv_w, conv_b, conv_ln_w, conv_ln_b, w_conv_proj, w_out, out):
    ctx = ExitStack()
    with ctx:
        def sb(name, shape, dt=F32, stack=ctx):
            return stack.enter_context(nc.sbuf_tensor(name, shape, dt))

        def sem(name):
            return ctx.enter_context(nc.semaphore(name))

        bank = [ctx.enter_context(nc.psum_tensor(f"bank{i}", [P, HALF], F32)) for i in range(8)]
        proj_bank, aux, s_bank, pt_bank, o_bank = bank[0:2], bank[2], bank[3:5], bank[5:7], bank[7]

        o_dram = [nc.dram_tensor(f"o_dram{g}", [PAIRS, T, OW], F32, kind="Internal") for g in (1, 2)]
        part_dram = nc.dram_tensor("part_dram", [KB, P, T], F32, kind="Internal")

        h_hi = sb("h_hi", [P, KB, T], F32R)
        h_lo = sb("h_lo", [P, KB, T], F32R)
        raw = sb("raw", [P, RAW, 1024])
        w_hi = sb("w_hi", [P, WR, 1024], F32R)
        w_lo = sb("w_lo", [P, WR, 1024], F32R)
        attn = sb("attn", [P, NT, CW])
        sg = sb("sg", [P, 4, HALF])
        gate_bc = sb("gate_bc", [P, D])
        ident = sb("ident", [P, P])
        ones_w = sb("ones_w", [P, P])
        mean_w = sb("mean_w", [P, P])
        head_w = sb("head_w", [P, P])
        mask = sb("mask", [P, 2 * P])
        mask2 = sb("mask2", [P, P])
        cols = sb("cols", [P, 72])
        conv_col = sb("conv_col", [P, CB, TAPS])
        eps = sb("eps", [P, 1])
        small = sb("small", [P, 40])
        cmb = sb("cmb", [P, 5, NT, 2])

        with ExitStack() as s:
            xt = sb("xt", [P, NT, D], stack=s)
            ada_w = sb("ada_w", [P, 3, 2 * D], stack=s)
            ada_part = sb("ada_part", [P, 2 * D], stack=s)
            junk = sb("junk", [P, D], stack=s)
            h32 = sb("h32", [P, 2, HALF], stack=s)
            rows = sb("rows", [72, P], stack=s)
            conv_rows = sb("conv_rows", [TAPS, CW], stack=s)
        with ExitStack() as s:
            glu = sb("glu", [P, 2, PAD + T], stack=s)
            acc_b = sb("acc_b", [P, T], stack=s)
            cv = sb("cv", [P, CB, T], stack=s)
            zc = sb("zc", [P, CB, T], stack=s)
            c_hi = sb("c_hi", [P, CB, T], F32R, stack=s)
            c_lo = sb("c_lo", [P, CB, T], F32R, stack=s)
        with ExitStack() as s:
            qT = sb("qT", [P, 2, T], stack=s)
            kT = sb("kT", [P, 2, T], stack=s)
            vT = sb("vT", [P, T], stack=s)
            v = sb("v", [P, NT, P], stack=s)
            qk_raw = sb("qk_raw", [P, 2, HALF], stack=s)
            rstd = sb("rstd", [P, 2, HALF], stack=s)
            probs = sb("probs", [P, 2, 2 * 2 * P], stack=s)
            pT = sb("pT", [P, 2, 4 * P], stack=s)
            o_own = [sb(f"o_own{i}", [P, NT, OW], stack=s) for i in range(4)]
            o_nat = [sb(f"o_nat{i}", [P, NT, OW], stack=s) for i in range(2)]
            negmax = sb("negmax", [P, 2, 2], stack=s)
        with ExitStack() as s:
            z_silu = sb("z_silu", [P, 2, HALF], stack=s)
            a32 = sb("a32", [P, 2, HALF], stack=s)
            a_hi = sb("a_hi", [P, CB, T], F32R, stack=s)
            a_lo = sb("a_lo", [P, CB, T], F32R, stack=s)
            merged = sb("merged", [P, KB, T], stack=s)
        y32 = a32

        names = """rows_in ada_used consts cols_ready sc_ready ones_ready part_done ada_cols
            mod_ready gate_mm gate_ready x_scaled xt_ready h_copied h_ready w_split w_hi_done
            pj_ready glu_in glu_ready conv_done mean_ready centered sq_ready var_ready ln_r ln_scaled
            ln_silu ln_z c_hi_done c_ready z_in sg_ready part_made
            qk_copied sq_in ss_ready rstd_done qk_ready vt_ready vtr_ready v_ready
            s_ready smax_done exp_done pt_ready pt_out o_ready o_out o_sent1 o_sent2 nat_in
            comb_d comb_e comb_w comb_done ln_done tr_ready zs_ready a32_made a_hi_done a_ready
            y_made merged_ready m_hi_done m_ready out_ready out_full out_scaled out_made
            gate_bias rstd_x xsq dve_chain act_chain pool_chain pe_seen conv_part""".split()
        S = {n: sem(n) for n in names}
        pj_free = [sem("pj_free0"), sem("pj_free1")]
        x_in = [sem(f"x_in{i}") for i in range(NT // 2)]
        ada_in = [sem(f"ada_in{i}") for i in range(3)]
        gate_in = [sem(f"gate_in{i}") for i in range(3)]
        raw_in = [sem(f"raw_in{i}") for i in range(RAW)]
        part_out = [sem(f"part_out{i}") for i in range(4)]
        part_back = [sem(f"part_back{i}") for i in range(KB)]
        x_again = [sem(f"x_again{i}") for i in range(4)]
        stored = [sem(f"stored{i}") for i in range(4)]

        w_in3 = w_in[0].rearrange("(k p) n -> p k n", p=P)
        proj3 = {"pA": w_attn_proj[0].rearrange("(k p) n -> p k n", p=P),
                 "pB": w_conv_proj[0].rearrange("(k p) n -> p k n", p=P)}
        wout3 = w_out[0].rearrange("(k p) n -> p k n", p=P)
        x3 = x[0].rearrange("(i p) d -> p i d", p=P)
        out3 = out[0].rearrange("(i p) d -> p i d", p=P)
        base = {"convb": UB0, "conva": UA0, "convz": ZC0, "gA": GA0, "gB": GB0, "z": ZA0}

        def block_source(n):
            kind, w = BLOCKS[n]
            r = raw[:, n % RAW, :]
            if kind == "out":
                nn, kk = divmod(w, 4)
                return (r.rearrange("p (k n) -> p k n", k=2),
                        wout3[:, 2 * kk:2 * kk + 2, nn * HALF:(nn + 1) * HALF])
            if kind in ("pA", "pB"):
                return r.rearrange("p (k n) -> p k n", k=CB), proj3[kind][:, :, 2 * P * w:2 * P * (w + 1)]
            if kind in ("q", "k", "v"):
                p, g = divmod(w, GROUPS)
                col = {"q": Q0, "k": K0, "v": V0}[kind] + g * CW + p * P
            else:
                col = base[kind] + w * P
            return r.rearrange("p (k n) -> p k n", k=KB), w_in3[:, :, col:col + P]

        def token_order(ap, g, tt):
            d = DILATION[g]
            n = HALF // d
            return ap.rearrange("p (r l) -> p l r", r=d)[:, n * tt:n * (tt + 1), :]

        def wait_copied(eng, key):
            eng.wait_ge(pj_free[SEG[key] % 2], SEG[key] // 2 + 1)

        def natural(ap, g):
            return ap.rearrange("p (l r) -> p l r", r=DILATION[g])

        def has_previous(g, i):
            return i >= 1 if g == 0 else i % 2 == 1 if g == 1 else False

        def out_tile(a):
            p, g = divmod(a, GROUPS)
            return o_own[p % 2] if g == 0 else o_own[1 + g]

        C_C, C_BADA, C_NORM, C_BG, C_CB, C_LW, C_LB, C_Q, C_K = 0, 8, 32, 40, 56, 60, 64, 68, 69
        NROWS = 70
        SC, SHIFT, SCALE_, SS, RS = 0, 8, 16, 24, 32
        gate_w = attn[:, 0:6, :].rearrange("p (a b) n -> p a (b n)", a=3)
        gate_part = attn[:, 6:8, :].rearrange("p b n -> p (b n)")

        def y_tile(k):
            return attn[:, k % 4, :]

        def x_tile(k):
            return attn[:, 4 + k % 4, :]

        def attn_transposes(pe, e):
            p, tt = divmod(e, 2)
            pe.wait_ge(S["comb_done"], p + 1)
            if e:
                pe.wait_ge(S["a32_made"], e)
            else:
                pe.wait_ge(S["v_ready"], 2 * STAGES)
            for i in range(4):
                ins = pe.transpose(aux[:, i * P:(i + 1) * P], attn[:, 4 * tt + i, p * P:(p + 1) * P], ident[:, :])
            ins.then_inc(S["tr_ready"], 1)

        def a_high(e, act):
            p, tt = divmod(e, 2)
            act.wait_ge(S["a32_made"], e + 1)
            act.activation(a_hi[:, p, tt * HALF:(tt + 1) * HALF], a32[:, e % 2, :], ACT.Copy).then_inc(S["a_hi_done"], 1)

        block = ctx.enter_context(nc.Block())

        @block.sync
        def _(sp):
            with nc.allow_non_contiguous_dma(reason="weight columns"):
                for i in range(0, NT, 2):
                    sp.dma_start(xt[:, i:i + 2, :], x3[:, i:i + 2, :]).then_inc(x_in[i // 2], 16)
                wa = w_ada[0].rearrange("(k p) n -> p k n", p=P)
                for k in range(KB):
                    if k >= 3:
                        sp.wait_ge(S["ada_used"], k - 2)
                    sp.dma_start(ada_w[:, k % 3, :], wa[:, k, 0:2 * D]).then_inc(ada_in[k % 3], 16)
                for n in range(RAW):
                    sp.dma_start(*block_source(n)).then_inc(raw_in[n % RAW], 16)
                for k in range(KB):
                    if k >= 3:
                        sp.wait_ge(S["ada_used"], KB + k - 2)
                    sp.dma_start(gate_w[:, k % 3, :], wa[:, k, 2 * D:3 * D]).then_inc(gate_in[k % 3], 16)

                natural_read = {NO[("q", 3 * p + 4)] + 4: p for p in range(PAIRS - 1)}
                natural_read[NO[("z", 0)] + 3] = PAIRS - 1
                for n in range(RAW, len(BLOCKS)):
                    sp.wait_ge(S["w_split"], n - RAW + 1)
                    sp.dma_start(*block_source(n)).then_inc(raw_in[n % RAW], 16)
                    if n in natural_read:
                        p = natural_read[n]
                        if p:
                            sp.wait_ge(S["comb_done"], p)
                        sp.wait_ge(S["o_sent1"], 32 * (p + 1))
                        sp.wait_ge(S["o_sent2"], 32 * (p + 1))
                        for g in range(2):
                            sp.dma_start(o_nat[g][:, :, :],
                                         o_dram[g].ap()[p].rearrange("(i p) w -> p i w", p=P)).then_inc(S["nat_in"], 16)
                    kind, w = BLOCKS[n]
                    if kind == "pA":
                        if w == 0:
                            for q in part_out:
                                sp.wait_ge(q, 32)
                            sp.wait_ge(S["comb_done"], PAIRS)
                        for j in (2 * w, 2 * w + 1):
                            sp.dma_start(merged[:, j, :], part_dram.ap()[j]).then_inc(part_back[j], 16)
                for k in range(16):
                    sp.wait_ge(S["out_made"], k + 1)
                    nn, t = divmod(k, NT)
                    sp.dma_start(out3[:, t, nn * HALF:(nn + 1) * HALF], y_tile(k)).then_inc(stored[k % 4], 16)
                for q in stored:
                    sp.wait_ge(q, 64)

        @block.gpsimd
        def _(pool):
            chain = [0]

            def link(ins):
                chain[0] += 1
                ins.then_inc(S["pool_chain"], 1)
                pool.wait_ge(S["pool_chain"], chain[0])

            link(pool.memset(ident[:, :], 0.0))
            link(pool.memset(mean_w[:, :], 1.0 / CW))
            link(pool.memset(ones_w[:, :], 1.0))
            link(pool.memset(eps[:, :], EPS))
            link(pool.memset(head_w[:, :], 0.0))
            link(pool.memset(mask[:, :], 0.0))
            link(pool.memset(mask2[:, :], 0.0))
            link(pool.affine_select(out=ident[:, :], in_=ident[:, :], compare_op=ALU.not_equal, fill=1.0,
                                    base=0, pattern=[[-1, P]], channel_multiplier=1))
            link(pool.memset(head_w[0:HD, 0:HD], 1.0 / HD))
            link(pool.memset(head_w[HD:P, HD:P], 1.0 / HD))
            link(pool.affine_select(out=mask[:, 0:P], in_=mask[:, 0:P], compare_op=ALU.is_ge, fill=MASKED,
                                    base=0, pattern=[[1, P]], channel_multiplier=-1))
            link(pool.affine_select(out=mask[:, P:2 * P], in_=mask[:, P:2 * P], compare_op=ALU.is_ge, fill=MASKED,
                                    base=0, pattern=[[-1, P]], channel_multiplier=1))
            link(pool.affine_select(out=mask2[:, :], in_=mask2[:, :], compare_op=ALU.is_ge, fill=MASKED,
                                    base=0, pattern=[[-1, P]], channel_multiplier=1))
            pool.memset(mask2[HD:P, 0:HD], MASKED).then_inc(S["consts"], 1)

            def split(n):
                pool.wait_ge(raw_in[n % RAW], 16 * (n // RAW + 1))
                if n >= WR:
                    if BLOCKS[n - WR][0] == "out":
                        nn, kk = divmod(BLOCKS[n - WR][1], 4)
                        if kk < 3:
                            pool.wait_ge(S["out_ready"], 3 * nn + kk + 1)
                        else:
                            pool.wait_ge(S["out_full"], NT * (nn + 1))
                    else:
                        pool.wait_ge(S["pj_ready"], LAST_SEG[n - WR] + 1)
                pool.tensor_copy(w_hi[:, n % WR, :], raw[:, n % RAW, :]).then_inc(S["w_hi_done"], 1)
                pool.wait_ge(S["w_hi_done"], n + 1)
                pool.tensor_tensor(w_lo[:, n % WR, :], raw[:, n % RAW, :], w_hi[:, n % WR, :].bitcast(F32),
                                   ALU.subtract).then_inc(S["w_split"], 1)

            def combine(p):
                pool.wait_ge(S["comb_w"], p + 1)
                tiles = [o_own[p % 2], o_nat[0], o_nat[1]]
                view = [t[:, :, 0:2 * HD].rearrange("p i (h d) -> p i h d", h=2) for t in tiles]
                for g in range(3):
                    w = cmb[:, 1 + g, :, :].unsqueeze(3).to_broadcast([P, NT, 2, HD])
                    ins = pool.tensor_tensor(view[g], view[g], w, ALU.mult)
                link(ins)
                link(pool.tensor_tensor(view[0], view[0], view[1], ALU.add))
                pool.tensor_tensor(attn[:, :, p * P:(p + 1) * P].rearrange("p i (h d) -> p i h d", h=2),
                                   view[0], view[2], ALU.add).then_inc(S["comb_done"], 1)

            for n in range(NO[("convz", 0)] + 1):
                split(n)
            for c in range(CB):
                if c >= 2:
                    pool.wait_ge(S["conv_done"], c - 1)
                else:
                    if c == 0:
                        pool.wait_ge(S["h_ready"], 16)
                    pool.memset(glu[:, c, 0:PAD], 0.0)
                for tt in range(2):
                    wait_copied(pool, ("convb", c, tt))
                    wait_copied(pool, ("conva", c, tt))
                    ins = pool.tensor_tensor(glu[:, c % 2, PAD + tt * HALF:PAD + (tt + 1) * HALF],
                                             sg[:, tt, :], sg[:, 2 + tt, :], ALU.mult)
                    ins.then_inc(S["glu_ready"], 1)
                if c + 1 < CB:
                    for n in range(3 * c + 3, 3 * c + 6):
                        split(n)
            for n in range(3 * CB, NO[("pB", 0)]):
                split(n)
            for tt in range(2):
                for c in range(CB):
                    pool.wait_ge(S["ln_silu"], CB * tt + c + 1)
                    half = slice(tt * HALF, (tt + 1) * HALF)
                    pool.tensor_tensor(cv[:, c, half], cv[:, c, half], zc[:, c, half],
                                       ALU.mult).then_inc(S["ln_z"], 1)
                for c in range(CB):
                    half = slice(tt * HALF, (tt + 1) * HALF)
                    pool.wait_ge(S["c_hi_done"], CB * tt + c + 1)
                    pool.tensor_tensor(c_lo[:, c, half], cv[:, c, half], c_hi[:, c, half].bitcast(F32),
                                       ALU.subtract).then_inc(S["c_ready"], 1)
            combine_after = {NO[("q", 3 * p + 4)] + 5: p for p in range(PAIRS - 1)}
            combine_after[NO[("z", 0)] + 4] = PAIRS - 1
            for n in range(NO[("pB", 0)], len(BLOCKS) - 1):
                split(n)
                if n in combine_after:
                    combine(combine_after[n])
            for k in range(16):
                if k == NT:
                    split(len(BLOCKS) - 1)
                pool.wait_ge(x_again[k % 4], 16 * (k // 4 + 1))
                pool.wait_ge(S["out_scaled"], k + 1)
                pool.tensor_tensor(y_tile(k), y_tile(k), x_tile(k), ALU.add).then_inc(S["out_made"], 1)

        @block.tensor
        def _(pe):
            w8 = [[w[:, i, :].rearrange("p (k n) -> p k n", k=KB) for i in range(WR)] for w in (w_hi, w_lo)]
            w4 = [[w[:, i, :].rearrange("p (k n) -> p k n", k=CB) for i in range(WR)] for w in (w_hi, w_lo)]
            w2 = [[w[:, i, :].rearrange("p (k n) -> p k n", k=2) for i in range(WR)] for w in (w_hi, w_lo)]

            def three(o, lh, ll, rh, rl, first, last):
                pe.matmul(o, lh, rh, start=first, stop=False)
                pe.matmul(o, lh, rl, start=False, stop=False)
                return pe.matmul(o, ll, rh, start=False, stop=last)

            def project(kind, w, tt, slot=None):
                n, s = NO[(kind, w)], SEG[(kind, w, tt)]
                pe.wait_ge(S["w_split"], n + 1)
                if s >= 2:
                    pe.wait_ge(pj_free[s % 2], s // 2)
                for k in range(KB):
                    cols_ = slice(tt * HALF, (tt + 1) * HALF)
                    ins = three(proj_bank[s % 2][:, :], w8[0][n % WR][:, k, :], w8[1][n % WR][:, k, :],
                                h_hi[:, k, cols_], h_lo[:, k, cols_], k == 0, k == KB - 1)
                    if k == KB - 1:
                        ins.then_inc(S["pj_ready"], 1)
                    if slot:
                        slot(k)

            def branch_out(kind, j, tt, hi, lo):
                n, s = NO[("p" + kind, j // 2)], SEG[("y" + kind, j, tt)]
                pe.wait_ge(S["w_split"], n + 1)
                pe.wait_ge(pj_free[s % 2], s // 2)
                for k in range(CB):
                    wc, tc = slice((j % 2) * P, (j % 2 + 1) * P), slice(tt * HALF, (tt + 1) * HALF)
                    ins = three(proj_bank[s % 2][:, :], w4[0][n % WR][:, k, wc], w4[1][n % WR][:, k, wc],
                                hi[:, k, tc], lo[:, k, tc], k == 0, k == CB - 1)
                ins.then_inc(S["pj_ready"], 1)

            pe.wait_ge(S["consts"], 1)
            pe.wait_ge(S["rows_in"], 16 * 10)
            pe.transpose(bank[0][:, 0:NROWS], rows[0:NROWS, :], ident[0:NROWS, 0:NROWS])
            for cc in range(CB):
                ins = pe.transpose(bank[0][:, 128 + 32 * cc:128 + 32 * cc + TAPS], conv_rows[:, cc * P:(cc + 1) * P],
                                   ident[0:TAPS, 0:TAPS])
            ins.then_inc(S["cols_ready"], 1)

            def x_transposes(m):
                tt, k = divmod(m, KB)
                pe.wait_ge(S["x_scaled"], 4 * tt + 4)
                if m >= 6:
                    pe.wait_ge(S["h_copied"], m - 5)
                for i in range(4):
                    ins = pe.transpose(bank[2 + m % 6][:, i * P:(i + 1) * P],
                                       xt[:, 4 * tt + i, k * P:(k + 1) * P], ident[:, :])
                ins.then_inc(S["xt_ready"], 1)

            for m in range(6):
                x_transposes(m)
            pe.wait_ge(S["ada_used"], KB)
            for q in range(16):
                ins = pe.matmul(bank[1][:, q:q + 1], ada_part[:, q * P:(q + 1) * P], ones_w[:, 0:1],
                                start=True, stop=True)
            ins.then_inc(S["ada_cols"], 1)
            for m in range(6, 16):
                x_transposes(m)
            pe.wait_ge(S["h_ready"], 16)
            pe.wait_ge(S["mod_ready"], 1)
            for cc in range(CB):
                for kind in ("convb", "conva", "convz"):
                    for tt in range(2):
                        project(kind, cc, tt)
                if cc == 0:
                    pe.wait_ge(S["ada_used"], 2 * KB)
                    for hh in range(2):
                        pe.matmul(bank[4 + hh][:, :], ones_w[:, :], gate_part[:, hh * HALF:(hh + 1) * HALF],
                                  start=True, stop=True).then_inc(S["gate_mm"], 1)
            for j in range(2):
                for tt in range(2):
                    project("gB", j, tt)
            pe.wait_ge(S["conv_done"], CB)
            pe.wait_ge(S["gate_ready"], 2)
            for tt in range(2):
                for cc in range(CB):
                    ins = pe.matmul(bank[2 + 2 * tt][:, :], mean_w[:, :], cv[:, cc, tt * HALF:(tt + 1) * HALF],
                                    start=(cc == 0), stop=(cc == CB - 1))
                ins.then_inc(S["mean_ready"], 1)
            for tt in range(2):
                for cc in range(CB):
                    pe.wait_ge(S["sq_ready"], CB * tt + cc + 1)
                    ins = pe.matmul(bank[3 + 2 * tt][:, :], mean_w[:, :], glu[:, 0, (cc % 2) * HALF:(cc % 2 + 1) * HALF],
                                    start=(cc == 0), stop=(cc == CB - 1))
                    ins.then_inc(S["var_ready"], 1)
            for i in range(KB // 2):
                if i:
                    for j in (2 * i, 2 * i + 1):
                        for tt in range(2):
                            project("gB", j, tt)
                for j in (2 * i, 2 * i + 1):
                    for tt in range(2):
                        if i == 0 and j == 0:
                            pe.wait_ge(S["c_ready"], CB * (tt + 1))
                        branch_out("B", j, tt, c_hi, c_lo)

            def attend(st, slot):
                a = st - 1
                g = a % GROUPS
                if slot in (3, 6):
                    hh = slot // 6
                    wait_copied(pe, ("v", a, 0))
                    wait_copied(pe, ("v", a, 1))
                    if hh:
                        pe.wait_ge(S["v_ready"], 2 * a + 1)
                    else:
                        pe.wait_ge(S["ln_done"], 4 * st if st < STAGES else 4 * STAGES)
                    for i in range(4):
                        t = 4 * hh + i
                        ins = pe.transpose(aux[:, i * P:(i + 1) * P], vT[:, t * P:(t + 1) * P], ident[:, :])
                    ins.then_inc(S["vtr_ready"], 1)
                if slot % 5 == 0 and slot // 5 < NT:
                    i = slot // 5
                    u = NT * a + i
                    if i == 0:
                        pe.wait_ge(S["qk_ready"], 4 * (a + 1))
                    if u:
                        pe.wait_ge(S["smax_done"], u)
                    first = i - 1 if has_previous(g, i) else i
                    n = (i + 1 - first) * P
                    for hh in range(2):
                        hp = slice(hh * HD, (hh + 1) * HD)
                        ins = pe.matmul(s_bank[hh][:, 0:n], qT[hp, a % 2, i * P:(i + 1) * P],
                                        kT[hp, a % 2, first * P:(i + 1) * P], start=True, stop=True)
                    ins.then_inc(S["s_ready"], 1)
                if slot % 5 == 0 and 1 <= slot // 5 <= NT:
                    i = slot // 5 - 1
                    u = NT * a + i
                    pe.wait_ge(S["exp_done"], u + 1)
                    if u >= 2:
                        pe.wait_ge(S["pt_out"], u - 1)
                    chunks = 2 if has_previous(g, i) else 1
                    for hh in range(2):
                        for b in range(chunks):
                            ins = pe.transpose(pt_bank[u % 2][:, (chunks * hh + b) * P:(chunks * hh + b + 1) * P],
                                               probs[:, u % 2, (2 * hh + b) * P:(2 * hh + b + 1) * P], ident[:, :])
                    ins.then_inc(S["pt_ready"], 1)
                if slot % 5 == 3 and 1 <= slot // 5 <= NT:
                    i = slot // 5 - 1
                    u = NT * a + i
                    pe.wait_ge(S["pt_out"], u + 1)
                    if i == 0:
                        pe.wait_ge(S["v_ready"], 2 * (a + 1))
                    if u:
                        pe.wait_ge(S["o_out"], u)
                    chunks = 2 if has_previous(g, i) else 1
                    for hh in range(2):
                        for b in range(chunks):
                            ins = pe.matmul(o_bank[:, hh * HD:(hh + 1) * HD],
                                            pT[:, u % 2, (chunks * hh + b) * P:(chunks * hh + b + 1) * P],
                                            v[:, i - chunks + 1 + b, hh * HD:(hh + 1) * HD],
                                            start=(b == 0), stop=(b == chunks - 1))
                    ins.then_inc(S["o_ready"], 1)

            def head_mean(st, m):
                pe.wait_ge(S["sq_in"], 4 * st + m + 1)
                if m:
                    pe.wait_ge(S["ln_done"], 4 * st + m)
                elif st:
                    pe.wait_ge(S["v_ready"], 2 * st)
                pe.matmul(aux[:, :], head_w[:, :], rstd[:, m % 2, :], start=True, stop=True).then_inc(S["ss_ready"], 1)

            for st in range(STAGES + 1):
                if st < STAGES:
                    halves = [(kind, st, tt) for kind in "qkv" for tt in range(2)]
                else:
                    halves = [("gA", j, tt) for j in range(2) for tt in range(2)]
                for m in range(6):
                    def slot(k):
                        if st:
                            attend(st, 8 * m + k)
                        if k == 3 and 1 <= m <= 4 and st < STAGES:
                            head_mean(st, m - 1)
                    if m < len(halves):
                        project(*halves[m], slot)
                    else:
                        for k in range(8):
                            slot(k)

            for p in range(PAIRS):
                for tt in range(2):
                    project("z", p, tt)
                    e = 2 * p + tt
                    if e < 2:
                        continue
                    attn_transposes(pe, e - 2)
            for e in (6, 7):
                attn_transposes(pe, e)
            for i in range(KB // 2):
                if i:
                    for j in (2 * i, 2 * i + 1):
                        for tt in range(2):
                            project("gA", j, tt)
                for j in (2 * i, 2 * i + 1):
                    for tt in range(2):
                        if i == 0 and j == 0:
                            pe.wait_ge(S["a_ready"], 8)
                        branch_out("A", j, tt, a_hi, a_lo)
            for nn in range(2):
                for kk in range(4):
                    n = NO[("out", 4 * nn + kk)]
                    pe.wait_ge(S["w_split"], n + 1)
                    for kb2 in range(2):
                        k = 2 * kk + kb2
                        if nn == 0:
                            pe.wait_ge(S["m_ready"], 2 * k + 2)
                        for t in range(NT):
                            if k == 0 and nn == 1:
                                pe.wait_ge(S["out_scaled"], t + 1)
                            if k == 0 and nn == 0 and t < 2:
                                wait_copied(pe, ("yA", KB - 1, t))
                            tc = slice(t * P, (t + 1) * P)
                            o = bank[t][:, :]
                            pe.matmul(o, h_hi[:, k, tc], w2[0][n % WR][:, kb2, :], start=(k == 0), stop=False)
                            pe.matmul(o, h_hi[:, k, tc], w2[1][n % WR][:, kb2, :], start=False, stop=False)
                            ins = pe.matmul(o, h_lo[:, k, tc], w2[0][n % WR][:, kb2, :], start=False, stop=(k == KB - 1))
                            if k == KB - 1:
                                ins.then_inc(S["out_full"], 1)
                            elif kb2 == 1 and t == NT - 1:
                                ins.then_inc(S["out_ready"], 1)

        @block.scalar
        def _(act):
            chain = [0]

            def link(ins):
                chain[0] += 1
                ins.then_inc(S["act_chain"], 1)
                act.wait_ge(S["act_chain"], chain[0])

            def rs(r, n, ap):
                act.dma_start(rows[r:r + n, :], ap).then_inc(S["rows_in"], 16)

            rs(C_C, 8, c[0].rearrange("(k p) -> k p", p=P))
            rs(C_BADA, 24, b_ada[0].rearrange("(k p) -> k p", p=P))
            rs(C_NORM, 8, norm_w[0].rearrange("(k p) -> k p", p=P))
            rs(C_BG, 16, b_gate[0].rearrange("(k p) -> k p", p=P))
            rs(C_CB, 4, conv_b[0].rearrange("(k p) -> k p", p=P))
            rs(C_LW, 4, conv_ln_w[0].rearrange("(k p) -> k p", p=P))
            rs(C_LB, 4, conv_ln_b[0].rearrange("(k p) -> k p", p=P))
            for r, ap in ((C_Q, q_norm_w), (C_K, k_norm_w)):
                act.dma_start(rows[r:r + 1, :].rearrange("a (b n) -> a b n", b=2),
                              ap.unsqueeze(1).to_broadcast([1, 2, HD])).then_inc(S["rows_in"], 16)
            act.dma_start(conv_rows[:, :], conv_w[0]).then_inc(S["rows_in"], 16)
            act.dma_start(gate_bc[:, :], b_ada[0:1, 2 * D:3 * D].to_broadcast([P, D])).then_inc(S["gate_bias"], 16)

            act.wait_ge(S["cols_ready"], 1)
            act.activation(cols[:, 0:NROWS], bank[0][:, 0:NROWS], ACT.Copy)
            link(act.activation(conv_col[:, :, :], bank[0][:, 128:256].rearrange("p (c k) -> p c k", k=32)[:, :, 0:TAPS],
                                ACT.Copy))
            act.activation(small[:, SC:SC + KB], cols[:, C_C:C_C + KB], ACT.Silu).then_inc(S["sc_ready"], 1)
            for i in range(NT):
                act.wait_ge(x_in[i // 2], 16)
                link(act.activation(junk[:, :], xt[:, i, :], ACT.Square, accum_out=small[:, SS + i:SS + i + 1]))
            act.activation(small[:, RS:RS + NT], small[:, SS:SS + NT], ACT.Sqrt, bias=eps[:, :],
                           scale=1.0 / D).then_inc(S["xsq"], 1)
            act.wait_ge(S["rstd_x"], 1)
            for i in range(NT):
                act.activation(xt[:, i, :], xt[:, i, :], ACT.Copy,
                               scale=small[:, SS + i:SS + i + 1]).then_inc(S["x_scaled"], 1)
            act.wait_ge(S["mod_ready"], 1)
            for m in range(16):
                tt, k = divmod(m, KB)
                act.wait_ge(S["xt_ready"], m + 1)
                if m >= 2:
                    act.wait_ge(S["h_ready"], m - 1)
                act.activation(h32[:, m % 2, :], bank[2 + m % 6][:, :], ACT.Identity,
                               scale=small[:, SCALE_ + k:SCALE_ + k + 1],
                               bias=small[:, SHIFT + k:SHIFT + k + 1]).then_inc(S["h_copied"], 1)

            def out_of(kind, w, tt, dst, func, **kw):
                s = SEG[(kind, w, tt)]
                act.wait_ge(S["pj_ready"], s + 1)
                return act.activation(dst, proj_bank[s % 2][:, :], func, **kw), pj_free[s % 2]

            for cc in range(CB):
                for kind, base_, func in (("convb", 0, ACT.Sigmoid), ("conva", 2, ACT.Copy)):
                    for tt in range(2):
                        if cc:
                            act.wait_ge(S["glu_ready"], 2 * (cc - 1) + tt + 1)
                        ins, free = out_of(kind, cc, tt, sg[:, base_ + tt, :], func)
                        ins.then_inc(free, 1)
                for tt in range(2):
                    if cc == 0 and tt == 0:
                        act.wait_ge(S["h_ready"], 16)
                    ins, free = out_of("convz", cc, tt, zc[:, cc, tt * HALF:(tt + 1) * HALF], ACT.Silu)
                    ins.then_inc(free, 1)

            def gate_sigmoid(kind, j, tt, col):
                if j >= 2:
                    wait_copied(act, ("y" + kind[1], j - 2, tt))
                ins, free = out_of(kind, j, tt, sg[:, 2 * (j % 2) + tt, :], ACT.Sigmoid,
                                   bias=cols[:, C_BG + col + j:C_BG + col + j + 1])
                ins.then_inc(free, 1)

            act.wait_ge(S["glu_ready"], 8)
            for j in range(2):
                for tt in range(2):
                    gate_sigmoid("gB", j, tt, KB)
            act.wait_ge(S["conv_done"], CB)
            for tt in range(2):
                half = slice(tt * HALF, (tt + 1) * HALF)
                for cc in range(CB):
                    act.wait_ge(S["centered"], CB * tt + cc + 1)
                    if CB * tt + cc >= 2:
                        act.wait_ge(S["var_ready"], CB * tt + cc - 1)
                    act.activation(glu[:, 0, (cc % 2) * HALF:(cc % 2 + 1) * HALF], cv[:, cc, half],
                                   ACT.Square).then_inc(S["sq_ready"], 1)
                act.wait_ge(S["var_ready"], CB * (tt + 1))
                r = glu[:, 1, tt * HALF:(tt + 1) * HALF]
                link(act.activation(r, bank[3 + 2 * tt][:, :], ACT.Ln, bias=eps[:, :]))
                act.activation(r, r, ACT.Exp, scale=-0.5).then_inc(S["ln_r"], 1)
            for tt in range(2):
                half = slice(tt * HALF, (tt + 1) * HALF)
                for cc in range(CB):
                    act.wait_ge(S["ln_scaled"], CB * tt + cc + 1)
                    act.activation(cv[:, cc, half], cv[:, cc, half], ACT.Silu,
                                   scale=cols[:, C_LW + cc:C_LW + cc + 1],
                                   bias=cols[:, C_LB + cc:C_LB + cc + 1]).then_inc(S["ln_silu"], 1)
                for cc in range(CB):
                    act.wait_ge(S["ln_z"], CB * tt + cc + 1)
                    act.activation(c_hi[:, cc, half], cv[:, cc, half], ACT.Copy).then_inc(S["c_hi_done"], 1)
            def send_parts(j0):
                for j in (j0, j0 + 1):
                    for tt in range(2):
                        wait_copied(act, ("yB", j, tt))
                    act.dma_start(part_dram.ap()[j], zc[:, j % 4, :]).then_inc(part_out[j % 4], 16)

            for i in range(1, KB // 2):
                for j in (2 * i, 2 * i + 1):
                    for tt in range(2):
                        gate_sigmoid("gB", j, tt, KB)
                send_parts(2 * i - 2)

            def exps(a, i):
                g = a % GROUPS
                u = NT * a + i
                act.wait_ge(S["smax_done"], u + 1)
                n = 2 * P if has_previous(g, i) else P
                o = out_tile(a)
                for hh in range(2):
                    pr = probs[:, u % 2, hh * 2 * P:hh * 2 * P + n]
                    ins = act.activation(pr, pr, ACT.Exp, bias=negmax[:, u % 2, hh:hh + 1],
                                         accum_out=o[:, i, 2 * HD + 2 + hh:2 * HD + 3 + hh])
                ins.then_inc(S["exp_done"], 1)

            def output(a, i):
                u = NT * a + i
                act.wait_ge(S["o_ready"], u + 1)
                act.activation(out_tile(a)[:, i, 0:2 * HD], o_bank[:, 0:2 * HD], ACT.Copy).then_inc(S["o_out"], 1)
                p, g = divmod(a, GROUPS)
                if g and i == NT - 1:
                    act.wait_ge(S["o_out"], u + 1)
                    o, dram, done = out_tile(a), o_dram[g - 1].ap()[p], S[f"o_sent{g}"]
                    if g == 1:
                        dst = dram.rearrange("(b l r) w -> b l r w", b=2, r=4)
                        for b in range(2):
                            act.dma_start(dst[b], o[:, b::2, :]).then_inc(done, 16)
                    else:
                        dst = dram.rearrange("(l i e) w -> e l i w", i=8, e=2)
                        for e in range(2):
                            act.dma_start(dst[e], o[e * HD:(e + 1) * HD, :, :]).then_inc(done, 16)

            qk_seen = [0]

            def take(st, m):
                g = st % GROUPS
                if m < 4:
                    k = 4 * st + m
                    if k >= 2:
                        act.wait_ge(S["qk_ready"], k - 1)
                    ins, free = out_of("qk"[m // 2], st, m % 2, qk_raw[:, m % 2, :], ACT.Copy)
                    ins.then_inc(free, 1)
                    act.wait_ge(free, SEG[("qk"[m // 2], st, m % 2)] // 2 + 1)
                    act.activation(rstd[:, m % 2, :], qk_raw[:, m % 2, :], ACT.Square).then_inc(S["sq_in"], 1)
                else:
                    if st and m == 4:
                        act.wait_ge(S["vtr_ready"], 2 * st)
                    s = SEG[("v", st, m - 4)]
                    act.wait_ge(S["pj_ready"], s + 1)
                    ins = act.activation(token_order(vT[:, :], g, m - 4), natural(proj_bank[s % 2][:, :], g), ACT.Copy)
                    ins.then_inc(pj_free[s % 2], 1)

            def head_rstd(st, m):
                act.wait_ge(S["ss_ready"], 4 * st + m + 1)
                r = rstd[:, m % 2, :]
                act.activation(r, aux[:, :], ACT.Ln, bias=eps[:, :]).then_inc(S["ln_done"], 1)
                act.wait_ge(S["ln_done"], 4 * st + m + 1)
                act.activation(r, r, ACT.Exp, scale=-0.5).then_inc(S["rstd_done"], 1)

            def values(a, hh):
                act.wait_ge(S["vtr_ready"], 2 * a + hh + 1)
                act.activation(v[:, 4 * hh:4 * hh + 4, :], aux[:, :].rearrange("p (i n) -> p i n", i=4),
                               ACT.Copy).then_inc(S["v_ready"], 1)

            def comb_exp(p):
                act.wait_ge(S["comb_d"], p + 1)
                act.activation(cmb[:, 1:4, :, :], cmb[:, 1:4, :, :], ACT.Exp).then_inc(S["comb_e"], 1)

            send_parts(KB - 2)
            for q in part_out:
                act.wait_ge(q, 32)
            for st in range(STAGES + 1):
                for slot in range(SLOTS):
                    m, k = divmod(slot, 8)
                    if k == 0:
                        if m == 0 and st:
                            take(st - 1, 5)
                        if 1 <= m and st < STAGES:
                            take(st, m - 1)
                        if 1 <= m <= 4 and st == STAGES:
                            gate_sigmoid("gA", (m - 1) // 2, (m - 1) % 2, 0)
                    if k == 4 and 1 <= m <= 4 and st < STAGES:
                        head_rstd(st, m - 1)
                    if not st:
                        continue
                    a = st - 1
                    if slot == 4:
                        values(a, 0)
                    if slot == 7:
                        values(a, 1)
                    if slot % 5 == 4:
                        i = slot // 5
                        if 1 <= i <= NT:
                            output(a, i - 1)
                        if i < NT:
                            exps(a, i)
                    if slot == 36 and st >= 4 and (st - 4) % 3 == 0:
                        comb_exp((st - 4) // 3)

            for e in range(8):
                p, tt = divmod(e, 2)
                if e >= 2:
                    act.wait_ge(S["a32_made"], e - 1)
                ins, free = out_of("z", p, tt, z_silu[:, e % 2, :], ACT.Silu)
                ins.then_inc(free, 1)
                if e >= 1:
                    a_high(e - 1, act)
                if e == 2:
                    comb_exp(PAIRS - 1)
            a_high(7, act)
            for i in range(1, KB // 2):
                for j in (2 * i, 2 * i + 1):
                    for tt in range(2):
                        gate_sigmoid("gA", j, tt, 0)
            act.wait_ge(S["pj_ready"], SEG[("gA", KB - 1, 1)] + 1)
            for k in range(KB):
                for tt in range(2):
                    act.wait_ge(S["merged_ready"], 2 * k + tt + 1)
                    act.activation(h_hi[:, k, tt * HALF:(tt + 1) * HALF], merged[:, k, tt * HALF:(tt + 1) * HALF],
                                   ACT.Copy).then_inc(S["m_hi_done"], 1)
            for k in range(16):
                nn, t = divmod(k, NT)
                if k >= 4:
                    act.wait_ge(S["out_made"], k - 3)
                else:
                    act.wait_ge(S["tr_ready"], 8)
                act.dma_start(x_tile(k), x3[:, t, nn * HALF:(nn + 1) * HALF]).then_inc(x_again[k % 4], 16)

        @block.vector
        def _(dve):
            chain = [0]

            def link(ins):
                chain[0] += 1
                ins.then_inc(S["dve_chain"], 1)
                dve.wait_ge(S["dve_chain"], chain[0])

            dve.wait_ge(S["sc_ready"], 1)
            for k in range(KB):
                dve.wait_ge(ada_in[k % 3], 16 * (k // 3 + 1))
                sc = small[:, SC + k:SC + k + 1]
                dst = ada_part[:, 0:2 * D]
                if k == 0:
                    ins = dve.tensor_scalar(dst, ada_w[:, 0, :], sc, None, ALU.mult)
                else:
                    ins = dve.scalar_tensor_tensor(dst, ada_w[:, k % 3, :], sc, dst, ALU.mult, ALU.add)
                ins.then_inc(S["ada_used"], 1)
                dve.wait_ge(S["ada_used"], k + 1)
                if k == 3:
                    dve.wait_ge(S["xsq"], 1)
                    dve.reciprocal(small[:, SS:SS + NT], small[:, RS:RS + NT]).then_inc(S["rstd_x"], 1)
            dve.wait_ge(S["ada_cols"], 1)
            link(dve.tensor_tensor(small[:, SHIFT:SHIFT + 16], bank[1][:, 0:16], cols[:, C_BADA:C_BADA + 16], ALU.add))
            dve.scalar_tensor_tensor(small[:, SCALE_:SCALE_ + KB], small[:, SCALE_:SCALE_ + KB], 1.0,
                                     cols[:, C_NORM:C_NORM + KB], ALU.add, ALU.mult).then_inc(S["mod_ready"], 1)
            for m in range(16):
                tt, k = divmod(m, KB)
                half = slice(tt * HALF, (tt + 1) * HALF)
                dve.wait_ge(S["h_copied"], m + 1)
                link(dve.tensor_copy(h_hi[:, k, half], h32[:, m % 2, :]))
                dve.tensor_tensor(h_lo[:, k, half], h32[:, m % 2, :], h_hi[:, k, half].bitcast(F32),
                                  ALU.subtract).then_inc(S["h_ready"], 1)
            for k in range(KB):
                dve.wait_ge(gate_in[k % 3], 16 * (k // 3 + 1))
                sc = small[:, SC + k:SC + k + 1]
                if k == 0:
                    ins = dve.tensor_scalar(gate_part, gate_w[:, 0, :], sc, None, ALU.mult)
                else:
                    ins = dve.scalar_tensor_tensor(gate_part, gate_w[:, k % 3, :], sc, gate_part, ALU.mult, ALU.add)
                ins.then_inc(S["ada_used"], 1)
                dve.wait_ge(S["ada_used"], KB + k + 1)
            link(dve.tensor_scalar(cols[:, C_Q:C_Q + 1], cols[:, C_Q:C_Q + 1], float(HD) ** -0.5, None, ALU.mult))
            for cc in range(CB):
                dve.wait_ge(S["glu_ready"], 2 * cc + 2)
                sums = [cv[:, cc, :], acc_b[:, :]]
                g_ = glu[:, cc % 2, :]
                for k in range(TAPS):
                    dst = sums[k % 2]
                    w = conv_col[:, cc, k:k + 1]
                    if k < 2:
                        ins = dve.tensor_scalar(dst, g_[:, k:k + T], w, None, ALU.mult)
                    else:
                        dve.wait_ge(S["conv_part"], TAPS * cc + k - 1)
                        ins = dve.scalar_tensor_tensor(dst, g_[:, k:k + T], w, dst, ALU.mult, ALU.add)
                    ins.then_inc(S["conv_part"], 1)
                dve.wait_ge(S["conv_part"], TAPS * (cc + 1))
                dve.scalar_tensor_tensor(sums[0], sums[0], cols[:, C_CB + cc:C_CB + cc + 1], sums[1],
                                         ALU.add, ALU.add).then_inc(S["conv_done"], 1)
                dve.wait_ge(S["conv_done"], cc + 1)
                if cc == 0:
                    dve.wait_ge(S["gate_bias"], 16)
                    for hh in range(2):
                        dve.wait_ge(S["gate_mm"], hh + 1)
                        gb = gate_bc[:, hh * HALF:(hh + 1) * HALF]
                        dve.tensor_tensor(gb, bank[4 + hh][:, :], gb, ALU.add).then_inc(S["gate_ready"], 1)

            for tt in range(2):
                dve.wait_ge(S["mean_ready"], tt + 1)
                for cc in range(CB):
                    half = cv[:, cc, tt * HALF:(tt + 1) * HALF]
                    dve.tensor_tensor(half, half, bank[2 + 2 * tt][:, :], ALU.subtract).then_inc(S["centered"], 1)
            for tt in range(2):
                dve.wait_ge(S["ln_r"], tt + 1)
                for cc in range(CB):
                    half = cv[:, cc, tt * HALF:(tt + 1) * HALF]
                    dve.tensor_tensor(half, half, glu[:, 1, tt * HALF:(tt + 1) * HALF],
                                      ALU.mult).then_inc(S["ln_scaled"], 1)
            for j in range(KB):
                for tt in range(2):
                    s = SEG[("yB", j, tt)]
                    k = 2 * j + tt
                    dve.wait_ge(S["pj_ready"], s + 1)
                    if k == 0:
                        dve.wait_ge(S["ln_z"], 2 * CB)
                    if k >= 8:
                        dve.wait_ge(part_out[j % 4], 16)
                    dst = zc[:, (k % 8) // 2, (k % 2) * HALF:(k % 2 + 1) * HALF]
                    ins = dve.tensor_tensor(dst, sg[:, 2 * (j % 2) + tt, :], proj_bank[s % 2][:, :], ALU.mult)
                    ins.then_inc(pj_free[s % 2], 1)

            def maxima(a, i):
                p, g = divmod(a, GROUPS)
                u = NT * a + i
                dve.wait_ge(S["s_ready"], u + 1)
                if u >= 2:
                    dve.wait_ge(S["pt_ready"], u - 1)
                if i == 0 and g == 0 and p >= 2:
                    dve.wait_ge(S["comb_done"], p - 1)
                if i == 0 and g and p:
                    dve.wait_ge(S[f"o_sent{g}"], 32 * p)
                o = out_tile(a)
                mk = mask2[:, :] if g == 2 else mask[:, :] if has_previous(g, i) else mask[:, P:2 * P]
                n = 2 * P if has_previous(g, i) else P
                for hh in range(2):
                    ins = dve.tensor_tensor_reduce(out=probs[:, u % 2, hh * 2 * P:hh * 2 * P + n],
                                                   in0=s_bank[hh][:, 0:n], in1=mk,
                                                   scale=1.0, scalar=-3e38, op0=ALU.add, op1=ALU.max,
                                                   accum_out=o[:, i, 2 * HD + hh:2 * HD + hh + 1])
                link(ins)
                dve.tensor_scalar(negmax[:, u % 2, :], o[:, i, 2 * HD:2 * HD + 2], -1.0, None,
                                  ALU.mult).then_inc(S["smax_done"], 1)

            def transposed(a, i):
                g = a % GROUPS
                u = NT * a + i
                dve.wait_ge(S["pt_ready"], u + 1)
                if u >= 2:
                    dve.wait_ge(S["o_ready"], u - 1)
                n = (4 if has_previous(g, i) else 2) * P
                dve.tensor_copy(pT[:, u % 2, 0:n], pt_bank[u % 2][:, 0:n]).then_inc(S["pt_out"], 1)

            def normalise(st, m):
                g = st % GROUPS
                dve.wait_ge(S["rstd_done"], 4 * st + m + 1)
                if st >= 2 and m == 0:
                    dve.wait_ge(S["s_ready"], NT * (st - 1))
                dst = (qT, kT)[m // 2][:, st % 2, :]
                col = (C_Q, C_K)[m // 2]
                dve.scalar_tensor_tensor(token_order(dst, g, m % 2), natural(qk_raw[:, m % 2, :], g),
                                         cols[:, col:col + 1], natural(rstd[:, m % 2, :], g),
                                         ALU.mult, ALU.mult).then_inc(S["qk_ready"], 1)

            def comb_small(p, part):
                ts = [o_own[p % 2], o_nat[0], o_nat[1]]
                mx = [t[:, :, 2 * HD:2 * HD + 2] for t in ts]
                dn = [t[:, :, 2 * HD + 2:2 * HD + 4] for t in ts]
                e = [cmb[:, 1 + g, :, :] for g in range(3)]
                top = cmb[:, 0, :, :]
                if part == 0:
                    dve.wait_ge(S["nat_in"], 32 * (p + 1))
                    if p:
                        dve.wait_ge(S["comb_done"], p)
                    dve.wait_ge(S["exp_done"], NT * (3 * p + 1))
                    link(dve.tensor_tensor(top, mx[0], mx[1], ALU.max))
                    link(dve.tensor_tensor(top, top, mx[2], ALU.max))
                    for g in range(3):
                        ins = dve.tensor_tensor(e[g], mx[g], top, ALU.subtract)
                    ins.then_inc(S["comb_d"], 1)
                else:
                    dve.wait_ge(S["comb_e"], p + 1)
                    t = cmb[:, 4, :, :]
                    link(dve.tensor_tensor(top, e[0], dn[0], ALU.mult))
                    for g in (1, 2):
                        link(dve.tensor_tensor(t, e[g], dn[g], ALU.mult))
                        link(dve.tensor_tensor(top, top, t, ALU.add))
                    link(dve.reciprocal(t, top))
                    for g in range(3):
                        ins = dve.tensor_tensor(e[g], e[g], t, ALU.mult)
                    ins.then_inc(S["comb_w"], 1)

            for st in range(STAGES + 1):
                for slot in range(SLOTS):
                    m, k = divmod(slot, 8)
                    if k == 6 and 1 <= m <= 4 and st < STAGES:
                        normalise(st, m - 1)
                    if not st:
                        continue
                    a = st - 1
                    if slot % 5 == 1:
                        i = slot // 5
                        if 1 <= i <= NT:
                            transposed(a, i - 1)
                        if i < NT:
                            maxima(a, i)
                    if st >= 4 and (st - 4) % 3 == 0:
                        if slot == 34:
                            comb_small((st - 4) // 3, 0)
                        if slot == 40:
                            comb_small((st - 4) // 3, 1)

            for e in range(8):
                p, tt = divmod(e, 2)
                half = slice(tt * HALF, (tt + 1) * HALF)
                if e == 2:
                    comb_small(PAIRS - 1, 0)
                    comb_small(PAIRS - 1, 1)
                dve.wait_ge(S["tr_ready"], e + 1)
                dve.wait_ge(pj_free[SEG[("z", p, tt)] % 2], SEG[("z", p, tt)] // 2 + 1)
                if e >= 2:
                    dve.wait_ge(S["a_ready"], e - 1)
                dve.tensor_tensor(a32[:, e % 2, :], aux[:, :], z_silu[:, e % 2, :], ALU.mult).then_inc(S["a32_made"], 1)
                dve.wait_ge(S["a_hi_done"], e + 1)
                dve.tensor_tensor(a_lo[:, p, half], a32[:, e % 2, :], a_hi[:, p, half].bitcast(F32),
                                  ALU.subtract).then_inc(S["a_ready"], 1)
            for j in range(KB):
                for tt in range(2):
                    s = SEG[("yA", j, tt)]
                    k = 2 * j + tt
                    half = slice(tt * HALF, (tt + 1) * HALF)
                    dve.wait_ge(S["pj_ready"], s + 1)
                    if k == 0:
                        dve.wait_ge(S["a_ready"], 8)
                    dst = y32[:, k % 2, :]
                    ins = dve.tensor_tensor(dst, sg[:, 2 * (j % 2) + tt, :], proj_bank[s % 2][:, :], ALU.mult)
                    ins.then_inc(pj_free[s % 2], 1)
                    wait_copied(dve, ("yA", j, tt))
                    dve.wait_ge(part_back[j], 16)
                    dve.tensor_tensor(merged[:, j, half], dst, merged[:, j, half], ALU.add).then_inc(S["merged_ready"], 1)
            for k in range(16):
                half = slice((k % 2) * HALF, (k % 2 + 1) * HALF)
                dve.wait_ge(S["m_hi_done"], k + 1)
                dve.tensor_tensor(h_lo[:, k // 2, half], merged[:, k // 2, half], h_hi[:, k // 2, half].bitcast(F32),
                                  ALU.subtract).then_inc(S["m_ready"], 1)
            for k in range(16):
                nn, t = divmod(k, NT)
                dve.wait_ge(S["out_full"], k + 1)
                if k >= 4:
                    dve.wait_ge(stored[k % 4], 16 * (k // 4))
                dve.tensor_tensor(y_tile(k), bank[t][:, :], gate_bc[:, nn * HALF:(nn + 1) * HALF],
                                  ALU.mult).then_inc(S["out_scaled"], 1)


_INS = ["x", "c", "w_ada", "b_ada", "norm_w", "w_in", "b_gate", "q_norm_w", "k_norm_w", "w_attn_proj",
        "conv_w", "conv_b", "conv_ln_w", "conv_ln_b", "w_conv_proj", "w_out"]


def kernel(**inputs):
    import numpy as _np
    import concourse.bacc as _bacc
    from concourse import mybir as _mybir
    from concourse.bass_utils import run_bass_kernel_spmd as _run

    nc = _bacc.Bacc("TRN2", target_bir_lowering=False, num_devices=1)
    arrays, args = {}, {}
    for name in _INS:
        a = _np.ascontiguousarray(inputs[name])
        arrays[f"in_{name}_dram"] = a
        args[name] = nc.dram_tensor(f"in_{name}_dram", a.shape, _mybir.dt.from_np(a.dtype), kind="ExternalInput").ap()
    args["out"] = nc.dram_tensor("out_0_dram", (1, 1024, 1024), _mybir.dt.float32, kind="ExternalOutput").ap()
    build(nc, **args)
    r = _run(nc, [arrays], core_ids=[0])
    return r.results[0]["out_0_dram"]
```

```python
from contextlib import ExitStack

import concourse.bass as bass
from concourse import mybir

P = 128
T = 1024
D = 1024
KB = D // P
NT = T // P
HALF = 512
CW = 512
CB = CW // P
TAPS = 31
PAD = TAPS - 1
HD = 64
PAIRS = 4
GROUPS = 3
DILATION = (1, 4, 16)
OW = 2 * HD + 4
EPS = 1e-6
MASKED = -1e30

Q0, K0, V0, ZA0, UA0, UB0, ZC0, GA0, GB0 = 0, 1536, 3072, 4608, 5120, 5632, 6144, 6656, 7680

F32 = mybir.dt.float32
F32R = mybir.dt.float32r
ALU = mybir.AluOpType
ACT = mybir.ActivationFunctionType

STAGES = PAIRS * GROUPS
SLOTS = 48


def blocks():
    out = []
    for c in range(CB):
        out += [("convb", c), ("conva", c), ("convz", c)]
    out += [("gB", j) for j in range(6)] + [("pB", i) for i in range(3)] + [("gB", 6), ("gB", 7), ("pB", 3)]
    for st in range(STAGES):
        out += [("q", st), ("k", st), ("v", st)]
    out += [("gA", 0), ("gA", 1)] + [("z", p) for p in range(PAIRS)] + [("pA", 0)]
    for i in range(1, KB // 2):
        out += [("gA", 2 * i), ("gA", 2 * i + 1), ("pA", i)]
    out += [("out", k) for k in range(8)]
    return out


BLOCKS = blocks()
NO = {b: n for n, b in enumerate(BLOCKS)}


def segments():
    seg, last = {}, {}
    for tt in range(2):
        for n in range(3):
            last[n] = seg[(*BLOCKS[n], tt)] = len(seg)
    for n, (kind, w) in enumerate(BLOCKS):
        if n < 3:
            continue
        if kind == "out":
            continue
        parts = [(kind, w)] if kind not in ("pA", "pB") else [("y" + kind[1], 2 * w), ("y" + kind[1], 2 * w + 1)]
        for part in parts:
            for tt in range(2):
                last[n] = seg[(*part, tt)] = len(seg)
    return seg, last


SEG, LAST_SEG = segments()
RAW, WR = 2, 3
GB_BEFORE = 2
POOL_TAPS = 8


def conv_halves(c):
    halves = [(kind, c, tt) for kind in ("convb", "conva", "convz") for tt in range(2)]
    return sorted(halves, key=lambda key: SEG[key])


def conv_schedule():
    keys = [key for c in range(CB) for key in conv_halves(c)] + [("gB", j, tt) for j in range(2) for tt in range(2)]
    steps = []
    for h, (kind, w, tt) in enumerate(keys):
        early = {0: 2, 3: 3, 4: 4}
        weights = early.get(h) if h < 6 else NO[(kind, w)] + 2 if tt == 0 else None
        c, at = divmod(h - 4, 6)
        spread = [[], [0, 1, 2, 3], [4], [5], [6], [7]] if c == 0 else [[0, 1], [2, 3], [4], [5], [6], [7]]
        steps.append((kind, w, tt, weights, [(c, i) for i in spread[at]] if h >= 4 else []))
    return steps


def build(nc, x, c, w_ada, b_ada, norm_w, w_in, b_gate, q_norm_w, k_norm_w, w_attn_proj,
          conv_w, conv_b, conv_ln_w, conv_ln_b, w_conv_proj, w_out, out):
    ctx = ExitStack()
    with ctx:
        def sb(name, shape, dt=F32, stack=ctx):
            return stack.enter_context(nc.sbuf_tensor(name, shape, dt))

        def sem(name):
            return ctx.enter_context(nc.semaphore(name))

        bank = [ctx.enter_context(nc.psum_tensor(f"bank{i}", [P, HALF], F32)) for i in range(8)]
        proj_bank, aux, s_bank, pt_bank, o_bank = bank[0:2], bank[2], bank[3:5], bank[5:7], bank[7]

        o_dram = [nc.dram_tensor(f"o_dram{g}", [PAIRS, T, OW], F32, kind="Internal") for g in (1, 2)]
        part_dram = nc.dram_tensor("part_dram", [KB, P, T], F32, kind="Internal")

        h_hi = sb("h_hi", [P, KB, T], F32R)
        h_lo = sb("h_lo", [P, KB, T], F32R)
        raw = sb("raw", [P, RAW, 1024])
        w_hi = sb("w_hi", [P, WR, 1024], F32R)
        w_lo = sb("w_lo", [P, WR, 1024], F32R)
        attn = sb("attn", [P, NT, CW])
        sg = sb("sg", [P, 4, HALF])
        gate_bc = sb("gate_bc", [P, D])
        ident = sb("ident", [P, P])
        ones_w = sb("ones_w", [P, P])
        mean_w = sb("mean_w", [P, P])
        head_w = sb("head_w", [P, P])
        head_wr = sb("head_wr", [P, P], F32R)
        mask = sb("mask", [P, 2 * P])
        mask2 = sb("mask2", [P, P])
        cols = sb("cols", [P, 72])
        conv_col = sb("conv_col", [P, CB, TAPS])
        eps = sb("eps", [P, 1])
        small = sb("small", [P, 40])
        cmb = sb("cmb", [P, 5, NT, 2])

        with ExitStack() as s:
            xt = sb("xt", [P, NT, D], stack=s)
            ada_w = sb("ada_w", [P, 3, 2 * D], stack=s)
            ada_part = sb("ada_part", [P, 2 * D], stack=s)
            junk = sb("junk", [P, D], stack=s)
            h32 = sb("h32", [P, 2, HALF], stack=s)
            rows = sb("rows", [72, P], stack=s)
            conv_rows = sb("conv_rows", [TAPS, CW], stack=s)
        with ExitStack() as s:
            glu = sb("glu", [P, 2, PAD + T], stack=s)
            acc_b = sb("acc_b", [P, T], stack=s)
            cv = sb("cv", [P, CB, T], stack=s)
            zc = sb("zc", [P, CB, T], stack=s)
            with ExitStack() as s2:
                tap_sum = sb("tap_sum", [P, 2, T], stack=s2)
                tap = sb("tap", [P, 2, T], stack=s2)
            c_hi = sb("c_hi", [P, CB, T], F32R, stack=s)
            c_lo = sb("c_lo", [P, CB, T], F32R, stack=s)
        with ExitStack() as s:
            qT = sb("qT", [P, 2, T], stack=s)
            kT = sb("kT", [P, 2, T], stack=s)
            vT = sb("vT", [P, T], stack=s)
            v = sb("v", [P, NT, P], stack=s)
            qk_raw = sb("qk_raw", [P, 2, HALF], stack=s)
            rstd = sb("rstd", [P, 2, HALF], stack=s)
            sq_hi = sb("sq_hi", [P, 2, HALF], F32R, stack=s)
            sq_lo = sb("sq_lo", [P, 2, HALF], F32R, stack=s)
            probs = sb("probs", [P, 2, 2 * 2 * P], stack=s)
            pT = sb("pT", [P, 2, 4 * P], stack=s)
            o_own = [sb(f"o_own{i}", [P, NT, OW], stack=s) for i in range(4)]
            o_nat = [sb(f"o_nat{i}", [P, NT, OW], stack=s) for i in range(2)]
            negmax = sb("negmax", [P, 2, 2], stack=s)
        with ExitStack() as s:
            z_silu = sb("z_silu", [P, 2, HALF], stack=s)
            a32 = sb("a32", [P, 2, HALF], stack=s)
            a_hi = sb("a_hi", [P, CB, T], F32R, stack=s)
            a_lo = sb("a_lo", [P, CB, T], F32R, stack=s)
            merged = sb("merged", [P, KB, T], stack=s)
        with ExitStack() as s:
            y_out = sb("y_out", [P, NT, HALF], stack=s)
        y32 = a32

        names = """ga_sigmoid sq_hi_done sq_lo_done tap_made tap_added rows_in ada_used consts cols_ready sc_ready ones_ready part_done ada_cols
            mod_ready gate_mm gate_ready x_scaled xt_ready h_copied h_ready w_split w_hi_done
            pj_ready glu_in glu_ready conv_done mean_ready centered sq_ready var_ready ln_r ln_scaled
            ln_silu ln_z c_hi_done c_ready z_in sg_ready part_made
            qk_copied sq_in ss_ready rstd_done qk_ready vt_ready vtr_ready v_ready
            s_ready smax_done exp_done pt_ready pt_out o_ready o_out o_sent1 o_sent2 nat_in
            comb_d comb_e comb_w comb_done ln_done tr_ready zs_ready a32_made a_hi_done a_ready
            y_made merged_ready m_hi_done m_ready out_ready out_full out_scaled
            gate_bias rstd_x xsq dve_chain act_chain pool_chain pe_seen conv_part""".split()
        S = {n: sem(n) for n in names}
        pj_free = [sem("pj_free0"), sem("pj_free1")]
        x_in = [sem(f"x_in{i}") for i in range(NT // 2)]
        ada_in = [sem(f"ada_in{i}") for i in range(3)]
        gate_in = [sem(f"gate_in{i}") for i in range(3)]
        raw_in = [sem(f"raw_in{i}") for i in range(RAW)]
        part_out = [sem(f"part_out{i}") for i in range(4)]
        part_back = [sem(f"part_back{i}") for i in range(KB)]
        x_again = [sem(f"x_again{i}") for i in range(NT)]
        out_made = [sem("out_made0"), sem("out_made1")]
        stored = [sem(f"stored{i}") for i in range(NT)]

        w_in3 = w_in[0].rearrange("(k p) n -> p k n", p=P)
        proj3 = {"pA": w_attn_proj[0].rearrange("(k p) n -> p k n", p=P),
                 "pB": w_conv_proj[0].rearrange("(k p) n -> p k n", p=P)}
        wout3 = w_out[0].rearrange("(k p) n -> p k n", p=P)
        x3 = x[0].rearrange("(i p) d -> p i d", p=P)
        out3 = out[0].rearrange("(i p) d -> p i d", p=P)
        base = {"convb": UB0, "conva": UA0, "convz": ZC0, "gA": GA0, "gB": GB0, "z": ZA0}

        def block_source(n):
            kind, w = BLOCKS[n]
            r = raw[:, n % RAW, :]
            if kind == "out":
                nn, kk = divmod(w, 4)
                return (r.rearrange("p (k n) -> p k n", k=2),
                        wout3[:, 2 * kk:2 * kk + 2, nn * HALF:(nn + 1) * HALF])
            if kind in ("pA", "pB"):
                return r.rearrange("p (k n) -> p k n", k=CB), proj3[kind][:, :, 2 * P * w:2 * P * (w + 1)]
            if kind in ("q", "k", "v"):
                p, g = divmod(w, GROUPS)
                col = {"q": Q0, "k": K0, "v": V0}[kind] + g * CW + p * P
            else:
                col = base[kind] + w * P
            return r.rearrange("p (k n) -> p k n", k=KB), w_in3[:, :, col:col + P]

        def token_order(ap, g, tt):
            d = DILATION[g]
            n = HALF // d
            return ap.rearrange("p (r l) -> p l r", r=d)[:, n * tt:n * (tt + 1), :]

        def wait_copied(eng, key):
            eng.wait_ge(pj_free[SEG[key] % 2], SEG[key] // 2 + 1)

        def natural(ap, g):
            return ap.rearrange("p (l r) -> p l r", r=DILATION[g])

        def has_previous(g, i):
            return i >= 1 if g == 0 else i % 2 == 1 if g == 1 else False

        def out_tile(a):
            p, g = divmod(a, GROUPS)
            return o_own[p % 2] if g == 0 else o_own[1 + g]

        C_C, C_BADA, C_NORM, C_BG, C_CB, C_LW, C_LB, C_Q, C_K = 0, 8, 32, 40, 56, 60, 64, 68, 69
        NROWS = 70
        SC, SHIFT, SCALE_, SS, RS = 0, 8, 16, 24, 32
        gate_w = attn[:, 0:6, :].rearrange("p (a b) n -> p a (b n)", a=3)
        gate_part = attn[:, 6:8, :].rearrange("p b n -> p (b n)")

        def gate_tile(kind, j, tt):
            if kind == "gB" and 2 <= j < 6:
                return attn[:, 2 * (j - 2) + tt, :]
            return sg[:, 2 * (j % 2) + tt, :]

        def square_tile(cc):
            return (glu[:, 0, :], acc_b[:, :])[cc // 2][:, (cc % 2) * HALF:(cc % 2 + 1) * HALF]

        def y_tile(k):
            return y_out[:, k % NT, :]

        def x_tile(k):
            return attn[:, k % NT, :]

        def attn_transposes(pe, e):
            p, tt = divmod(e, 2)
            pe.wait_ge(S["comb_done"], p + 1)
            if e >= 2:
                pe.wait_ge(S["a32_made"], e - 1)
            elif e == 1:
                pe.wait_ge(S["smax_done"], NT * STAGES)
            else:
                pe.wait_ge(S["v_ready"], 2 * STAGES)
            for i in range(4):
                ins = pe.transpose(bank[2 + e % 2][:, i * P:(i + 1) * P], attn[:, 4 * tt + i, p * P:(p + 1) * P], ident[:, :])
            ins.then_inc(S["tr_ready"], 1)

        def a_high(e, act):
            p, tt = divmod(e, 2)
            act.wait_ge(S["a32_made"], e + 1)
            act.activation(a_hi[:, p, tt * HALF:(tt + 1) * HALF], a32[:, e % 2, :], ACT.Copy).then_inc(S["a_hi_done"], 1)

        block = ctx.enter_context(nc.Block())

        @block.sync
        def _(sp):
            with nc.allow_non_contiguous_dma(reason="weight columns"):
                def load_x(i):
                    sp.dma_start(xt[:, 2 * i:2 * i + 2, :], x3[:, 2 * i:2 * i + 2, :]).then_inc(x_in[i], 16)

                def load_block(n):
                    sp.dma_start(*block_source(n)).then_inc(raw_in[n % RAW], 16)

                load_x(0)
                load_x(1)
                wa = w_ada[0].rearrange("(k p) n -> p k n", p=P)
                for k in range(KB):
                    if k >= 3:
                        sp.wait_ge(S["ada_used"], k - 2)
                    sp.dma_start(ada_w[:, k % 3, :], wa[:, k, 0:2 * D]).then_inc(ada_in[k % 3], 16)
                    if k == KB - 3:
                        load_block(0)
                load_block(1)
                load_x(2)
                load_x(3)
                gate_loads = {NO[("q", 0)] + 1: (0, 1, 2), NO[("q", 0)] + 2: (3, 4),
                              NO[("q", 0)] + 3: (5, 6), NO[("q", 0)] + 4: (7,)}
                natural_read = {NO[("q", 3 * p + 4)] + 4: p for p in range(PAIRS - 1)}
                natural_read[NO[("z", 0)] + 4] = PAIRS - 1
                for n in range(RAW, len(BLOCKS)):
                    sp.wait_ge(S["w_split"], n - RAW + 1)
                    load_block(n)
                    for k in gate_loads.get(n, ()):
                        if k == 0:
                            wait_copied(sp, ("yB", 5, 0))
                            wait_copied(sp, ("yB", 5, 1))
                        if k >= 3:
                            sp.wait_ge(S["ada_used"], KB + k - 2)
                        sp.dma_start(gate_w[:, k % 3, :], wa[:, k, 2 * D:3 * D]).then_inc(gate_in[k % 3], 16)
                    if n in natural_read:
                        p = natural_read[n]
                        if p:
                            sp.wait_ge(S["comb_done"], p)
                        sp.wait_ge(S["o_sent1"], 32 * (p + 1))
                        sp.wait_ge(S["o_sent2"], 32 * (p + 1))
                        for g in range(2):
                            sp.dma_start(o_nat[g][:, :, :],
                                         o_dram[g].ap()[p].rearrange("(i p) w -> p i w", p=P)).then_inc(S["nat_in"], 16)
                    kind, w = BLOCKS[n - 1]
                    if kind == "pA":
                        if w == 0:
                            for q in part_out:
                                sp.wait_ge(q, 32)
                            sp.wait_ge(S["comb_done"], PAIRS)
                        for j in (2 * w, 2 * w + 1):
                            sp.dma_start(merged[:, j, :], part_dram.ap()[j]).then_inc(part_back[j], 16)
                for k in range(16):
                    sp.wait_ge(out_made[k % 2], k // 2 + 1)
                    nn, t = divmod(k, NT)
                    sp.dma_start(out3[:, t, nn * HALF:(nn + 1) * HALF], y_tile(k)).then_inc(stored[k % NT], 16)
                for q in stored:
                    sp.wait_ge(q, 32)

        @block.gpsimd
        def _(pool):
            chain = [0]

            def link(ins):
                chain[0] += 1
                ins.then_inc(S["pool_chain"], 1)
                pool.wait_ge(S["pool_chain"], chain[0])

            link(pool.memset(ident[:, :], 0.0))
            link(pool.memset(mean_w[:, :], 1.0 / CW))
            link(pool.memset(ones_w[:, :], 1.0))
            link(pool.memset(eps[:, :], EPS))
            link(pool.memset(head_w[:, :], 0.0))
            link(pool.memset(mask[:, :], 0.0))
            link(pool.memset(mask2[:, :], 0.0))
            link(pool.affine_select(out=ident[:, :], in_=ident[:, :], compare_op=ALU.not_equal, fill=1.0,
                                    base=0, pattern=[[-1, P]], channel_multiplier=1))
            link(pool.memset(head_w[0:HD, 0:HD], 1.0 / HD))
            link(pool.memset(head_w[HD:P, HD:P], 1.0 / HD))
            link(pool.affine_select(out=mask[:, 0:P], in_=mask[:, 0:P], compare_op=ALU.is_ge, fill=MASKED,
                                    base=0, pattern=[[1, P]], channel_multiplier=-1))
            link(pool.affine_select(out=mask[:, P:2 * P], in_=mask[:, P:2 * P], compare_op=ALU.is_ge, fill=MASKED,
                                    base=0, pattern=[[-1, P]], channel_multiplier=1))
            link(pool.affine_select(out=mask2[:, :], in_=mask2[:, :], compare_op=ALU.is_ge, fill=MASKED,
                                    base=0, pattern=[[-1, P]], channel_multiplier=1))
            link(pool.tensor_copy(head_wr[:, :], head_w[:, :]))
            pool.memset(mask2[HD:P, 0:HD], MASKED).then_inc(S["consts"], 1)

            def split(n):
                pool.wait_ge(S["w_hi_done"], n + 1)
                pool.tensor_tensor(w_lo[:, n % WR, :], raw[:, n % RAW, :], w_hi[:, n % WR, :].bitcast(F32),
                                   ALU.subtract).then_inc(S["w_split"], 1)

            def combine(p):
                pool.wait_ge(S["comb_w"], p + 1)
                tiles = [o_own[p % 2], o_nat[0], o_nat[1]]
                view = [t[:, :, 0:2 * HD].rearrange("p i (h d) -> p i h d", h=2) for t in tiles]
                for g in range(3):
                    w = cmb[:, 1 + g, :, :].unsqueeze(3).to_broadcast([P, NT, 2, HD])
                    ins = pool.tensor_tensor(view[g], view[g], w, ALU.mult)
                link(ins)
                link(pool.tensor_tensor(view[0], view[0], view[1], ALU.add))
                pool.tensor_tensor(attn[:, :, p * P:(p + 1) * P].rearrange("p i (h d) -> p i h d", h=2),
                                   view[0], view[2], ALU.add).then_inc(S["comb_done"], 1)

            split(0)
            split(1)
            pool_first = NO[("gB", 1)] + 3
            for kind, c, tt, weights, taps in conv_schedule():
                if kind == "conva":
                    if c >= 2:
                        pool.wait_ge(S["conv_done"], c - 1)
                    elif tt == 0:
                        if c == 0:
                            pool.wait_ge(S["h_ready"], 16)
                        pool.memset(glu[:, c, 0:PAD], 0.0)
                    wait_copied(pool, ("convb", c, tt))
                    wait_copied(pool, ("conva", c, tt))
                    pool.tensor_tensor(glu[:, c % 2, PAD + tt * HALF:PAD + (tt + 1) * HALF],
                                       sg[:, tt, :], sg[:, 2 + tt, :], ALU.mult).then_inc(S["glu_ready"], 1)
                if weights:
                    split(weights)
                for tc, i in taps:
                    if i == 0:
                        continue
                    t = (POOL_TAPS - 1) * tc + i - 1
                    pool.wait_ge(S["tap_made"], POOL_TAPS * tc + i + 1)
                    if t:
                        pool.wait_ge(S["tap_added"], t)
                    pool.tensor_tensor(tap_sum[:, tc % 2, :], tap_sum[:, tc % 2, :], tap[:, t % 2, :],
                                       ALU.add).then_inc(S["tap_added"], 1)
            for n in range(pool_first, NO[("pB", 2)] + 1):
                split(n)
            combine_after = {NO[("q", 3 * p + 4)] + 5: p for p in range(PAIRS - 1)}
            combine_after[NO[("z", 0)] + 4] = PAIRS - 1
            def square_low(st, m):
                pool.wait_ge(S["sq_hi_done"], 4 * st + m + 1)
                pool.tensor_tensor(sq_lo[:, m % 2, :], rstd[:, m % 2, :], sq_hi[:, m % 2, :].bitcast(F32),
                                   ALU.subtract).then_inc(S["sq_lo_done"], 1)

            for n in range(NO[("pB", 2)] + 1, len(BLOCKS) - 1):
                kind, st = BLOCKS[n - 2]
                if kind in ("q", "k"):
                    square_low(st, 2 * "qk".index(kind))
                split(n)
                if kind in ("q", "k"):
                    square_low(st, 2 * "qk".index(kind) + 1)
                if n in combine_after:
                    combine(combine_after[n])
            for k in range(16):
                if k == NT:
                    split(len(BLOCKS) - 1)
                if k >= NT and k % 2:
                    continue
                pool.wait_ge(x_again[k % NT], 16 * (k // NT + 1))
                pool.wait_ge(S["out_scaled"], k + 1)
                pool.tensor_tensor(y_tile(k), y_tile(k), x_tile(k), ALU.add).then_inc(out_made[k % 2], 1)

        @block.tensor
        def _(pe):
            w8 = [[w[:, i, :].rearrange("p (k n) -> p k n", k=KB) for i in range(WR)] for w in (w_hi, w_lo)]
            w4 = [[w[:, i, :].rearrange("p (k n) -> p k n", k=CB) for i in range(WR)] for w in (w_hi, w_lo)]
            w2 = [[w[:, i, :].rearrange("p (k n) -> p k n", k=2) for i in range(WR)] for w in (w_hi, w_lo)]

            def three(o, lh, ll, rh, rl, first, last):
                pe.matmul(o, lh, rh, start=first, stop=False)
                pe.matmul(o, lh, rl, start=False, stop=False)
                return pe.matmul(o, ll, rh, start=False, stop=last)

            def project(kind, w, tt, slot=None, before=None):
                n, s = NO[(kind, w)], SEG[(kind, w, tt)]
                pe.wait_ge(S["w_split"], n + 1)
                if s >= 2:
                    pe.wait_ge(pj_free[s % 2], s // 2)
                for k in range(KB):
                    if before:
                        before(k)
                    cols_ = slice(tt * HALF, (tt + 1) * HALF)
                    ins = three(proj_bank[s % 2][:, :], w8[0][n % WR][:, k, :], w8[1][n % WR][:, k, :],
                                h_hi[:, k, cols_], h_lo[:, k, cols_], k == 0, k == KB - 1)
                    if k == KB - 1:
                        ins.then_inc(S["pj_ready"], 1)
                    if slot:
                        slot(k)

            def branch_out(kind, j, tt, hi, lo):
                n, s = NO[("p" + kind, j // 2)], SEG[("y" + kind, j, tt)]
                pe.wait_ge(S["w_split"], n + 1)
                pe.wait_ge(pj_free[s % 2], s // 2)
                for k in range(CB):
                    if kind == "A" and j == 0:
                        pe.wait_ge(S["a_ready"], 2 * k + tt + 1)
                    wc, tc = slice((j % 2) * P, (j % 2 + 1) * P), slice(tt * HALF, (tt + 1) * HALF)
                    ins = three(proj_bank[s % 2][:, :], w4[0][n % WR][:, k, wc], w4[1][n % WR][:, k, wc],
                                hi[:, k, tc], lo[:, k, tc], k == 0, k == CB - 1)
                ins.then_inc(S["pj_ready"], 1)

            pe.wait_ge(S["consts"], 1)
            pe.wait_ge(S["rows_in"], 16 * 10)
            pe.transpose(bank[0][:, 0:NROWS], rows[0:NROWS, :], ident[0:NROWS, 0:NROWS])
            for cc in range(CB):
                ins = pe.transpose(bank[0][:, 128 + 32 * cc:128 + 32 * cc + TAPS], conv_rows[:, cc * P:(cc + 1) * P],
                                   ident[0:TAPS, 0:TAPS])
            ins.then_inc(S["cols_ready"], 1)

            def x_transposes(m):
                tt, k = divmod(m, KB)
                pe.wait_ge(S["x_scaled"], 4 * tt + 4)
                if m >= 6:
                    pe.wait_ge(S["h_copied"], m - 5)
                for i in range(4):
                    ins = pe.transpose(bank[2 + m % 6][:, i * P:(i + 1) * P],
                                       xt[:, 4 * tt + i, k * P:(k + 1) * P], ident[:, :])
                ins.then_inc(S["xt_ready"], 1)

            for m in range(6):
                x_transposes(m)
            pe.wait_ge(S["ada_used"], KB)
            for q in range(16):
                ins = pe.matmul(bank[1][:, q:q + 1], ada_part[:, q * P:(q + 1) * P], ones_w[:, 0:1],
                                start=True, stop=True)
            ins.then_inc(S["ada_cols"], 1)
            x_transposes(6)
            x_transposes(7)
            pe.wait_ge(S["mod_ready"], 1)
            for cc in range(CB):
                for h_no, key in enumerate(conv_halves(cc)):
                    def before(k):
                        if cc == 0 and h_no in (0, 3):
                            pe.wait_ge(S["h_ready"], KB * key[2] + k + 1)
                        if cc == 0 and h_no == 1 and k == KB - 1:
                            for m in range(8, 14):
                                x_transposes(m)
                        if cc == 0 and h_no == 2 and k in (5, 6):
                            x_transposes(9 + k)
                    project(*key, before=before)
            for j in range(GB_BEFORE):
                for tt in range(2):
                    project("gB", j, tt)
            pe.wait_ge(S["conv_done"], CB)
            for tt in range(2):
                for cc in range(CB):
                    ins = pe.matmul(bank[2 + 2 * tt][:, :], mean_w[:, :], cv[:, cc, tt * HALF:(tt + 1) * HALF],
                                    start=(cc == 0), stop=(cc == CB - 1))
                ins.then_inc(S["mean_ready"], 1)

            def variance(tt, cc):
                pe.wait_ge(S["sq_ready"], CB * tt + cc + 1)
                pe.matmul(bank[3 + 2 * tt][:, :], mean_w[:, :], square_tile(cc),
                          start=(cc == 0), stop=(cc == CB - 1)).then_inc(S["var_ready"], 1)

            for j in range(GB_BEFORE, 6):
                for tt in range(2):
                    v_half = 2 * (j - GB_BEFORE) + tt - 1
                    project("gB", j, tt, slot=lambda k: variance(v_half, k // 2) if v_half in (0, 1) and k % 2 else None)
            for i in range(KB // 2):
                if i == 3:
                    for j in (6, 7):
                        for tt in range(2):
                            project("gB", j, tt)
                for j in (2 * i, 2 * i + 1):
                    for tt in range(2):
                        if i == 0 and j == 0:
                            pe.wait_ge(S["c_ready"], CB * (tt + 1))
                        branch_out("B", j, tt, c_hi, c_lo)

            def attend(st, slot):
                a = st - 1
                g = a % GROUPS
                if slot in (3, 6):
                    hh = slot // 6
                    wait_copied(pe, ("v", a, 0))
                    wait_copied(pe, ("v", a, 1))
                    if hh:
                        pe.wait_ge(S["v_ready"], 2 * a + 1)
                    else:
                        pe.wait_ge(S["ln_done"], 4 * st if st < STAGES else 4 * STAGES)
                    for i in range(4):
                        t = 4 * hh + i
                        ins = pe.transpose(aux[:, i * P:(i + 1) * P], vT[:, t * P:(t + 1) * P], ident[:, :])
                    ins.then_inc(S["vtr_ready"], 1)
                if slot % 5 == 0 and slot // 5 < NT:
                    i = slot // 5
                    u = NT * a + i
                    if i == 0:
                        pe.wait_ge(S["qk_ready"], 4 * (a + 1))
                    if u:
                        pe.wait_ge(S["smax_done"], u)
                    first = i - 1 if has_previous(g, i) else i
                    n = (i + 1 - first) * P
                    for hh in range(2):
                        hp = slice(hh * HD, (hh + 1) * HD)
                        ins = pe.matmul(s_bank[hh][:, 0:n], qT[hp, a % 2, i * P:(i + 1) * P],
                                        kT[hp, a % 2, first * P:(i + 1) * P], start=True, stop=True)
                    ins.then_inc(S["s_ready"], 1)
                if slot % 5 == 2 and 1 <= slot // 5 <= NT:
                    i = slot // 5 - 1
                    u = NT * a + i
                    pe.wait_ge(S["exp_done"], u + 1)
                    if u == 0:
                        pe.wait_ge(S["gate_ready"], 2)
                    if u >= 2:
                        pe.wait_ge(S["pt_out"], u - 1)
                    chunks = 2 if has_previous(g, i) else 1
                    for hh in range(2):
                        for b in range(chunks):
                            ins = pe.transpose(pt_bank[u % 2][:, (chunks * hh + b) * P:(chunks * hh + b + 1) * P],
                                               probs[:, u % 2, (2 * hh + b) * P:(2 * hh + b + 1) * P], ident[:, :])
                    ins.then_inc(S["pt_ready"], 1)
                if slot % 5 == 4 and 1 <= slot // 5 <= NT:
                    i = slot // 5 - 1
                    u = NT * a + i
                    pe.wait_ge(S["pt_out"], u + 1)
                    if i == 0:
                        pe.wait_ge(S["v_ready"], 2 * (a + 1))
                    if u:
                        pe.wait_ge(S["o_out"], u)
                    chunks = 2 if has_previous(g, i) else 1
                    for hh in range(2):
                        for b in range(chunks):
                            ins = pe.matmul(o_bank[:, hh * HD:(hh + 1) * HD],
                                            pT[:, u % 2, (chunks * hh + b) * P:(chunks * hh + b + 1) * P],
                                            v[:, i - chunks + 1 + b, hh * HD:(hh + 1) * HD],
                                            start=(b == 0), stop=(b == chunks - 1))
                    ins.then_inc(S["o_ready"], 1)

            def head_mean(st, m):
                pe.wait_ge(S["sq_lo_done"], 4 * st + m + 1)
                if m:
                    pe.wait_ge(S["ln_done"], 4 * st + m)
                elif st:
                    pe.wait_ge(S["v_ready"], 2 * st)
                pe.matmul(aux[:, :], head_wr[:, :], sq_hi[:, m % 2, :], start=True, stop=False)
                pe.matmul(aux[:, :], head_wr[:, :], sq_lo[:, m % 2, :], start=False, stop=True).then_inc(S["ss_ready"], 1)

            for st in range(STAGES + 1):
                if st < STAGES:
                    halves = [(kind, st, tt) for kind in "qkv" for tt in range(2)]
                else:
                    halves = [(kind, j, tt) for kind, j in (("gA", 0), ("gA", 1), ("z", 0)) for tt in range(2)]
                for m in range(6):
                    def slot(k):
                        if st:
                            attend(st, 8 * m + k)
                        if k == 5 and 1 <= m <= 4 and st < STAGES:
                            head_mean(st, m - 1)
                        if st == 0 and m == 5 and k == 6:
                            pe.wait_ge(S["ada_used"], 2 * KB)
                            for hh in range(2):
                                pe.matmul(pt_bank[hh][:, :], ones_w[:, :], gate_part[:, hh * HALF:(hh + 1) * HALF],
                                          start=True, stop=True).then_inc(S["gate_mm"], 1)
                    project(*halves[m], slot)

            for p in range(1, PAIRS):
                for tt in range(2):
                    project("z", p, tt)
                    attn_transposes(pe, 2 * p + tt - 2)
            for e in (6, 7):
                attn_transposes(pe, e)
            for i in range(KB // 2):
                if i:
                    for j in (2 * i, 2 * i + 1):
                        for tt in range(2):
                            project("gA", j, tt)
                for j in (2 * i, 2 * i + 1):
                    for tt in range(2):
                        branch_out("A", j, tt, a_hi, a_lo)
            for nn in range(2):
                for kk in range(4):
                    n = NO[("out", 4 * nn + kk)]
                    pe.wait_ge(S["w_split"], n + 1)
                    for kb2 in range(2):
                        k = 2 * kk + kb2
                        if nn == 0:
                            pe.wait_ge(S["m_ready"], 2 * k + 2)
                        for t in range(NT):
                            if k == 0 and nn == 1:
                                pe.wait_ge(S["out_scaled"], t + 1)
                            if k == 0 and nn == 0 and t < 2:
                                wait_copied(pe, ("yA", KB - 1, t))
                            tc = slice(t * P, (t + 1) * P)
                            o = bank[t][:, :]
                            pe.matmul(o, h_hi[:, k, tc], w2[0][n % WR][:, kb2, :], start=(k == 0), stop=False)
                            pe.matmul(o, h_hi[:, k, tc], w2[1][n % WR][:, kb2, :], start=False, stop=False)
                            ins = pe.matmul(o, h_lo[:, k, tc], w2[0][n % WR][:, kb2, :], start=False, stop=(k == KB - 1))
                            if k == KB - 1:
                                ins.then_inc(S["out_full"], 1)
                            elif kb2 == 1 and t == NT - 1:
                                ins.then_inc(S["out_ready"], 1)

        @block.scalar
        def _(act):
            chain = [0]

            def link(ins):
                chain[0] += 1
                ins.then_inc(S["act_chain"], 1)
                act.wait_ge(S["act_chain"], chain[0])

            def rs(r, n, ap):
                act.dma_start(rows[r:r + n, :], ap).then_inc(S["rows_in"], 16)

            rs(C_C, 8, c[0].rearrange("(k p) -> k p", p=P))
            rs(C_BADA, 24, b_ada[0].rearrange("(k p) -> k p", p=P))
            rs(C_NORM, 8, norm_w[0].rearrange("(k p) -> k p", p=P))
            rs(C_BG, 16, b_gate[0].rearrange("(k p) -> k p", p=P))
            rs(C_CB, 4, conv_b[0].rearrange("(k p) -> k p", p=P))
            rs(C_LW, 4, conv_ln_w[0].rearrange("(k p) -> k p", p=P))
            rs(C_LB, 4, conv_ln_b[0].rearrange("(k p) -> k p", p=P))
            for r, ap in ((C_Q, q_norm_w), (C_K, k_norm_w)):
                act.dma_start(rows[r:r + 1, :].rearrange("a (b n) -> a b n", b=2),
                              ap.unsqueeze(1).to_broadcast([1, 2, HD])).then_inc(S["rows_in"], 16)
            act.dma_start(conv_rows[:, :], conv_w[0]).then_inc(S["rows_in"], 16)
            act.dma_start(gate_bc[:, :], b_ada[0:1, 2 * D:3 * D].to_broadcast([P, D])).then_inc(S["gate_bias"], 16)

            act.wait_ge(S["cols_ready"], 1)
            act.activation(cols[:, 0:NROWS], bank[0][:, 0:NROWS], ACT.Copy)
            link(act.activation(conv_col[:, :, :], bank[0][:, 128:256].rearrange("p (c k) -> p c k", k=32)[:, :, 0:TAPS],
                                ACT.Copy))
            act.activation(small[:, SC:SC + KB], cols[:, C_C:C_C + KB], ACT.Silu).then_inc(S["sc_ready"], 1)
            def w_high(n):
                act.wait_ge(raw_in[n % RAW], 16 * (n // RAW + 1))
                if n >= WR:
                    if BLOCKS[n - WR][0] == "out":
                        nn, kk = divmod(BLOCKS[n - WR][1], 4)
                        if kk < 3:
                            act.wait_ge(S["out_ready"], 3 * nn + kk + 1)
                        else:
                            act.wait_ge(S["out_full"], NT * (nn + 1))
                    else:
                        act.wait_ge(S["pj_ready"], LAST_SEG[n - WR] + 1)
                act.activation(w_hi[:, n % WR, :], raw[:, n % RAW, :], ACT.Copy).then_inc(S["w_hi_done"], 1)

            def x_stats(i0):
                for i in range(i0, i0 + 4):
                    act.wait_ge(x_in[i // 2], 16)
                    link(act.activation(junk[:, :], xt[:, i, :], ACT.Square, accum_out=small[:, SS + i:SS + i + 1]))
                act.activation(small[:, RS + i0:RS + i0 + 4], small[:, SS + i0:SS + i0 + 4], ACT.Sqrt, bias=eps[:, :],
                               scale=1.0 / D).then_inc(S["xsq"], 1)

            def h_out(tt):
                for k in range(KB):
                    m = KB * tt + k
                    act.wait_ge(S["xt_ready"], m + 1)
                    if m >= 2:
                        act.wait_ge(S["h_ready"], m - 1)
                    for dst in (h_hi[:, k, tt * HALF:(tt + 1) * HALF], h32[:, m % 2, :])[k % 2:]:
                        ins = act.activation(dst, bank[2 + m % 6][:, :], ACT.Identity,
                                             scale=small[:, SCALE_ + k:SCALE_ + k + 1],
                                             bias=small[:, SHIFT + k:SHIFT + k + 1])
                    ins.then_inc(S["h_copied"], 1)

            def out_of(kind, w, tt, dst, func, **kw):
                s = SEG[(kind, w, tt)]
                act.wait_ge(S["pj_ready"], s + 1)
                return act.activation(dst, proj_bank[s % 2][:, :], func, **kw), pj_free[s % 2]

            def conv_input(kind, cc, tt):
                if kind == "convz":
                    ins, free = out_of("convz", cc, tt, zc[:, cc, tt * HALF:(tt + 1) * HALF], ACT.Silu)
                else:
                    base_, func = (0, ACT.Sigmoid) if kind == "convb" else (2, ACT.Copy)
                    if cc:
                        act.wait_ge(S["glu_ready"], 2 * (cc - 1) + tt + 1)
                    ins, free = out_of(kind, cc, tt, sg[:, base_ + tt, :], func)
                ins.then_inc(free, 1)

            x_stats(0)
            act.wait_ge(S["rstd_x"], 1)
            for i in range(4):
                act.activation(xt[:, i, :], xt[:, i, :], ACT.Copy,
                               scale=small[:, SS + i:SS + i + 1]).then_inc(S["x_scaled"], 1)
            w_high(0)
            act.wait_ge(S["mod_ready"], 1)
            h_out(0)
            w_high(1)
            x_stats(4)
            conv_input(*conv_halves(0)[0])
            w_high(2)
            conv_input(*conv_halves(0)[1])
            h_out(1)
            act.wait_ge(S["h_ready"], 16)

            def next_weights(kind, w, tt):
                if tt == 0:
                    w_high(NO[(kind, w)] + 2)

            def tap_product(c, i):
                k = TAPS - POOL_TAPS + i
                act.wait_ge(S["glu_ready"], 2 * c + 2)
                t = (POOL_TAPS - 1) * c + i - 1
                if i == 0 and c >= 2:
                    act.wait_ge(S["conv_done"], c - 1)
                if i and t >= 2:
                    act.wait_ge(S["tap_added"], t - 1)
                dst = tap[:, t % 2, :] if i else tap_sum[:, c % 2, :]
                bias = {} if i else {"bias": cols[:, C_CB + c:C_CB + c + 1]}
                act.activation(dst, glu[:, c % 2, k:k + T], ACT.Identity, scale=conv_col[:, c, k:k + 1],
                               **bias).then_inc(S["tap_made"], 1)

            def gate_sigmoid(kind, j, tt, col):
                if kind == "gA" and j >= 2:
                    wait_copied(act, ("yA", j - 2, tt))
                if kind == "gB" and j >= 6:
                    wait_copied(act, ("yB", j - 6, tt))
                ins, free = out_of(kind, j, tt, gate_tile(kind, j, tt), ACT.Sigmoid,
                                   bias=cols[:, C_BG + col + j:C_BG + col + j + 1])
                ins.then_inc(free, 1)
                next_weights(kind, j, tt)

            for step, (kind, ch, tt, weights, taps) in enumerate(conv_schedule()):
                if step >= 2:
                    if kind == "gB":
                        if (ch, tt) == (0, 0):
                            act.wait_ge(S["glu_ready"], 2 * CB)
                        gate_sigmoid(kind, ch, tt, KB)
                    else:
                        conv_input(kind, ch, tt)
                        if weights:
                            w_high(weights)
                for tap_ in taps:
                    tap_product(*tap_)

            def ln_squares(tt):
                for cc in range(CB):
                    act.wait_ge(S["centered"], CB * tt + cc + 1)
                    if tt:
                        act.wait_ge(S["var_ready"], cc + 1)
                    act.activation(square_tile(cc), cv[:, cc, tt * HALF:(tt + 1) * HALF],
                                   ACT.Square).then_inc(S["sq_ready"], 1)

            def ln_rstd(tt):
                act.wait_ge(S["var_ready"], CB * (tt + 1))
                r = glu[:, 1, tt * HALF:(tt + 1) * HALF]
                act.preload_act_table_set("natural_log_exp_and_others")
                link(act.activation(r, bank[3 + 2 * tt][:, :], ACT.Ln, bias=eps[:, :]))
                act.activation(r, r, ACT.Exp, scale=-0.5).then_inc(S["ln_r"], 1)

            def ln_swish(tt):
                for cc in range(CB):
                    half = cv[:, cc, tt * HALF:(tt + 1) * HALF]
                    act.wait_ge(S["ln_scaled"], CB * tt + cc + 1)
                    act.activation(half, half, ACT.Silu, scale=cols[:, C_LW + cc:C_LW + cc + 1],
                                   bias=cols[:, C_LB + cc:C_LB + cc + 1]).then_inc(S["ln_silu"], 1)

            def c_high(tt):
                for cc in range(CB):
                    half = slice(tt * HALF, (tt + 1) * HALF)
                    act.wait_ge(S["ln_z"], CB * tt + cc + 1)
                    act.activation(c_hi[:, cc, half], cv[:, cc, half], ACT.Copy).then_inc(S["c_hi_done"], 1)

            ln_squares(0)
            gate_sigmoid("gB", 2, 0, KB)
            ln_squares(1)
            gate_sigmoid("gB", 2, 1, KB)
            ln_rstd(0)
            gate_sigmoid("gB", 3, 0, KB)
            ln_rstd(1)
            gate_sigmoid("gB", 3, 1, KB)
            ln_swish(0)
            gate_sigmoid("gB", 4, 0, KB)
            c_high(0)
            gate_sigmoid("gB", 4, 1, KB)
            ln_swish(1)
            gate_sigmoid("gB", 5, 0, KB)
            c_high(1)
            gate_sigmoid("gB", 5, 1, KB)

            def send_parts(j0):
                for j in (j0, j0 + 1):
                    for tt in range(2):
                        wait_copied(act, ("yB", j, tt))
                    act.dma_start(part_dram.ap()[j], zc[:, j % 4, :]).then_inc(part_out[j % 4], 16)

            w_high(NO[("pB", 2)])
            w_high(NO[("pB", 2)] + 1)
            send_parts(0)
            w_high(NO[("pB", 2)] + 2)
            send_parts(2)
            for j in (6, 7):
                for tt in range(2):
                    gate_sigmoid("gB", j, tt, KB)
            send_parts(4)
            w_high(NO[("q", 0)] + 1)
            def exps(a, i):
                g = a % GROUPS
                u = NT * a + i
                act.wait_ge(S["smax_done"], u + 1)
                n = 2 * P if has_previous(g, i) else P
                o = out_tile(a)
                for hh in range(2):
                    pr = probs[:, u % 2, hh * 2 * P:hh * 2 * P + n]
                    ins = act.activation(pr, pr, ACT.Exp, bias=negmax[:, u % 2, hh:hh + 1],
                                         accum_out=o[:, i, 2 * HD + 2 + hh:2 * HD + 3 + hh])
                ins.then_inc(S["exp_done"], 1)

            def output(a, i):
                u = NT * a + i
                act.wait_ge(S["o_ready"], u + 1)
                act.activation(out_tile(a)[:, i, 0:2 * HD], o_bank[:, 0:2 * HD], ACT.Copy).then_inc(S["o_out"], 1)
                p, g = divmod(a, GROUPS)
                if g and i == NT - 1:
                    act.wait_ge(S["o_out"], u + 1)
                    o, dram, done = out_tile(a), o_dram[g - 1].ap()[p], S[f"o_sent{g}"]
                    if g == 1:
                        dst = dram.rearrange("(b l r) w -> b l r w", b=2, r=4)
                        for b in range(2):
                            act.dma_start(dst[b], o[:, b::2, :]).then_inc(done, 16)
                    else:
                        dst = dram.rearrange("(l i e) w -> e l i w", i=8, e=2)
                        for e in range(2):
                            act.dma_start(dst[e], o[e * HD:(e + 1) * HD, :, :]).then_inc(done, 16)

            def take_z(tt):
                if tt == 0:
                    act.wait_ge(S["qk_ready"], 4 * STAGES)
                ins, free = out_of("z", 0, tt, qk_raw[:, tt, :], ACT.Copy)
                ins.then_inc(free, 1)

            def take(st, m):
                g = st % GROUPS
                if m < 4:
                    k = 4 * st + m
                    if k >= 2:
                        act.wait_ge(S["qk_ready"], k - 1)
                    ins, free = out_of("qk"[m // 2], st, m % 2, qk_raw[:, m % 2, :], ACT.Copy)
                    ins.then_inc(free, 1)
                    act.wait_ge(free, SEG[("qk"[m // 2], st, m % 2)] // 2 + 1)
                    act.activation(rstd[:, m % 2, :], qk_raw[:, m % 2, :], ACT.Square)
                    act.activation(sq_hi[:, m % 2, :], qk_raw[:, m % 2, :], ACT.Square).then_inc(S["sq_hi_done"], 1)
                else:
                    if st and m == 4:
                        act.wait_ge(S["vtr_ready"], 2 * st)
                    s = SEG[("v", st, m - 4)]
                    act.wait_ge(S["pj_ready"], s + 1)
                    ins = act.activation(token_order(vT[:, :], g, m - 4), natural(proj_bank[s % 2][:, :], g), ACT.Copy)
                    ins.then_inc(pj_free[s % 2], 1)

            def head_rstd(st, m):
                act.wait_ge(S["ss_ready"], 4 * st + m + 1)
                r = rstd[:, m % 2, :]
                act.activation(r, aux[:, :], ACT.Ln, bias=eps[:, :]).then_inc(S["ln_done"], 1)
                act.wait_ge(S["ln_done"], 4 * st + m + 1)
                act.activation(r, r, ACT.Exp, scale=-0.5).then_inc(S["rstd_done"], 1)

            def values(a, hh):
                act.wait_ge(S["vtr_ready"], 2 * a + hh + 1)
                act.activation(v[:, 4 * hh:4 * hh + 4, :], aux[:, :].rearrange("p (i n) -> p i n", i=4),
                               ACT.Copy).then_inc(S["v_ready"], 1)

            def comb_exp(p):
                act.wait_ge(S["comb_d"], p + 1)
                act.activation(cmb[:, 1:4, :, :], cmb[:, 1:4, :, :], ACT.Exp).then_inc(S["comb_e"], 1)

            send_parts(KB - 2)
            for q in part_out:
                act.wait_ge(q, 32)
            act.preload_act_table_set("natural_log_exp_and_others")
            for st in range(STAGES + 1):
                for slot in range(SLOTS):
                    m, k = divmod(slot, 8)
                    if st and slot % 5 == 3 and slot // 5 < NT:
                        exps(st - 1, slot // 5)
                    if k == 2 and m % 2:
                        w_high(NO[("q", 0)] + 3 * st + m // 2 + 2)
                    if k == 0:
                        if m == 0 and st:
                            take(st - 1, 5)
                        if 1 <= m and st < STAGES:
                            take(st, m - 1)
                        if m == 5 and st == STAGES:
                            take_z(0)
                        if 1 <= m <= 4 and st == STAGES:
                            j, tt = divmod(m - 1, 2)
                            ins, free = out_of("gA", j, tt, gate_tile("gA", j, tt), ACT.Identity,
                                               bias=cols[:, C_BG + j:C_BG + j + 1])
                            ins.then_inc(free, 1)
                    if k == 6 and 1 <= m <= 4 and st < STAGES:
                        head_rstd(st, m - 1)
                    if not st:
                        continue
                    a = st - 1
                    if slot == 4:
                        values(a, 0)
                    if slot == 7:
                        values(a, 1)
                    if slot % 5 == 0 and slot // 5 >= 2:
                        output(a, slot // 5 - 2)
                    if slot == 36 and st >= 4 and (st - 4) % 3 == 0:
                        comb_exp((st - 4) // 3)

            for e in range(4):
                tile = sg[:, e, :]
                wait_copied(act, ("gA", e // 2, e % 2))
                act.activation(tile, tile, ACT.Sigmoid).then_inc(S["ga_sigmoid"], 1)
            take_z(1)
            for tt in range(2):
                wait_copied(act, ("z", 0, tt))
                act.activation(z_silu[:, tt, :], qk_raw[:, tt, :], ACT.Silu).then_inc(S["zs_ready"], 1)
            for e in range(8):
                p, tt = divmod(e, 2)
                if e >= 2:
                    act.wait_ge(S["a32_made"], e - 1)
                    ins, free = out_of("z", p, tt, z_silu[:, e % 2, :], ACT.Silu)
                    ins.then_inc(free, 1)
                    next_weights("z", p, tt)
                if e >= 1:
                    a_high(e - 1, act)
                if e == 2:
                    comb_exp(PAIRS - 1)
            a_high(7, act)
            w_high(NO[("pA", 0)] + 2)
            for i in range(1, KB // 2):
                for j in (2 * i, 2 * i + 1):
                    for tt in range(2):
                        gate_sigmoid("gA", j, tt, 0)
                w_high(NO[("pA", i)] + 2)

            def load_x_again(k):
                nn, t = divmod(k, NT)
                if k >= NT:
                    act.wait_ge(out_made[k % 2], (k - NT) // 2 + 1)
                act.dma_start(x_tile(k), x3[:, t, nn * HALF:(nn + 1) * HALF]).then_inc(x_again[k % NT], 16)

            act.wait_ge(S["tr_ready"], 8)
            for k in range(NT):
                load_x_again(k)
            act.wait_ge(S["pj_ready"], SEG[("gA", KB - 1, 1)] + 1)
            for k in range(KB):
                for tt in range(2):
                    act.wait_ge(S["merged_ready"], 2 * k + tt + 1)
                    act.activation(h_hi[:, k, tt * HALF:(tt + 1) * HALF], merged[:, k, tt * HALF:(tt + 1) * HALF],
                                   ACT.Copy).then_inc(S["m_hi_done"], 1)
            for n in range(NO[("out", 2)], NO[("out", 7)]):
                w_high(n)
            w_high(NO[("out", 7)])
            for k in range(NT, 2 * NT):
                load_x_again(k)

        @block.vector
        def _(dve):
            chain = [0]

            def link(ins):
                chain[0] += 1
                ins.then_inc(S["dve_chain"], 1)
                dve.wait_ge(S["dve_chain"], chain[0])

            dve.wait_ge(S["sc_ready"], 1)
            for k in range(KB):
                dve.wait_ge(ada_in[k % 3], 16 * (k // 3 + 1))
                sc = small[:, SC + k:SC + k + 1]
                dst = ada_part[:, 0:2 * D]
                if k == 0:
                    ins = dve.tensor_scalar(dst, ada_w[:, 0, :], sc, None, ALU.mult)
                else:
                    ins = dve.scalar_tensor_tensor(dst, ada_w[:, k % 3, :], sc, dst, ALU.mult, ALU.add)
                ins.then_inc(S["ada_used"], 1)
                dve.wait_ge(S["ada_used"], k + 1)
                if k == 3:
                    dve.wait_ge(S["xsq"], 1)
                    dve.reciprocal(small[:, SS:SS + 4], small[:, RS:RS + 4]).then_inc(S["rstd_x"], 1)
            dve.wait_ge(S["ada_cols"], 1)
            link(dve.tensor_tensor(small[:, SHIFT:SHIFT + 16], bank[1][:, 0:16], cols[:, C_BADA:C_BADA + 16], ALU.add))
            dve.scalar_tensor_tensor(small[:, SCALE_:SCALE_ + KB], small[:, SCALE_:SCALE_ + KB], 1.0,
                                     cols[:, C_NORM:C_NORM + KB], ALU.add, ALU.mult).then_inc(S["mod_ready"], 1)
            for m in range(16):
                tt, k = divmod(m, KB)
                half = slice(tt * HALF, (tt + 1) * HALF)
                if m == KB:
                    dve.wait_ge(S["xsq"], 2)
                    dve.reciprocal(small[:, SS + 4:SS + 8], small[:, RS + 4:RS + 8]).then_inc(S["rstd_x"], 1)
                    dve.wait_ge(S["rstd_x"], 2)
                    for i in range(4, NT):
                        dve.tensor_scalar(xt[:, i, :], xt[:, i, :], small[:, SS + i:SS + i + 1], None,
                                          ALU.mult).then_inc(S["x_scaled"], 1)
                dve.wait_ge(S["h_copied"], m + 1)
                if k % 2:
                    link(dve.tensor_copy(h_hi[:, k, half], h32[:, m % 2, :]))
                dve.tensor_tensor(h_lo[:, k, half], h32[:, m % 2, :], h_hi[:, k, half].bitcast(F32),
                                  ALU.subtract).then_inc(S["h_ready"], 1)
            link(dve.tensor_scalar(cols[:, C_Q:C_Q + 1], cols[:, C_Q:C_Q + 1], float(HD) ** -0.5, None, ALU.mult))
            dve_taps = TAPS - POOL_TAPS
            for cc in range(CB):
                dve.wait_ge(S["glu_ready"], 2 * cc + 2)
                sums = [cv[:, cc, :], acc_b[:, :]]
                g_ = glu[:, cc % 2, :]
                for k in range(dve_taps):
                    dst = sums[k % 2]
                    w = conv_col[:, cc, k:k + 1]
                    if k < 2:
                        ins = dve.tensor_scalar(dst, g_[:, k:k + T], w, None, ALU.mult)
                    else:
                        dve.wait_ge(S["conv_part"], (dve_taps + 1) * cc + k - 1)
                        ins = dve.scalar_tensor_tensor(dst, g_[:, k:k + T], w, dst, ALU.mult, ALU.add)
                    ins.then_inc(S["conv_part"], 1)
                dve.wait_ge(S["conv_part"], (dve_taps + 1) * cc + dve_taps)
                dve.tensor_tensor(sums[0], sums[0], sums[1], ALU.add).then_inc(S["conv_part"], 1)
                dve.wait_ge(S["conv_part"], (dve_taps + 1) * (cc + 1))
                dve.wait_ge(S["tap_added"], (POOL_TAPS - 1) * (cc + 1))
                dve.tensor_tensor(sums[0], sums[0], tap_sum[:, cc % 2, :], ALU.add).then_inc(S["conv_done"], 1)

            for tt in range(2):
                dve.wait_ge(S["mean_ready"], tt + 1)
                for cc in range(CB):
                    half = cv[:, cc, tt * HALF:(tt + 1) * HALF]
                    dve.tensor_tensor(half, half, bank[2 + 2 * tt][:, :], ALU.subtract).then_inc(S["centered"], 1)
            for tt in range(2):
                dve.wait_ge(S["ln_r"], tt + 1)
                for cc in range(CB):
                    half = cv[:, cc, tt * HALF:(tt + 1) * HALF]
                    dve.tensor_tensor(half, half, glu[:, 1, tt * HALF:(tt + 1) * HALF],
                                      ALU.mult).then_inc(S["ln_scaled"], 1)
            for tt in range(2):
                half = slice(tt * HALF, (tt + 1) * HALF)
                for cc in range(CB):
                    dve.wait_ge(S["ln_silu"], CB * tt + cc + 1)
                    dve.tensor_tensor(cv[:, cc, half], cv[:, cc, half], zc[:, cc, half],
                                      ALU.mult).then_inc(S["ln_z"], 1)
                for cc in range(CB):
                    dve.wait_ge(S["c_hi_done"], CB * tt + cc + 1)
                    dve.tensor_tensor(c_lo[:, cc, half], cv[:, cc, half], c_hi[:, cc, half].bitcast(F32),
                                      ALU.subtract).then_inc(S["c_ready"], 1)
            for j in range(KB):
                for tt in range(2):
                    s = SEG[("yB", j, tt)]
                    k = 2 * j + tt
                    dve.wait_ge(S["pj_ready"], s + 1)
                    if k == 0:
                        dve.wait_ge(S["ln_z"], 2 * CB)
                    if k >= 8:
                        dve.wait_ge(part_out[j % 4], 16)
                    dst = zc[:, (k % 8) // 2, (k % 2) * HALF:(k % 2 + 1) * HALF]
                    ins = dve.tensor_tensor(dst, gate_tile("gB", j, tt), proj_bank[s % 2][:, :], ALU.mult)
                    ins.then_inc(pj_free[s % 2], 1)

            def maxima(a, i):
                p, g = divmod(a, GROUPS)
                u = NT * a + i
                dve.wait_ge(S["s_ready"], u + 1)
                if u >= 2:
                    dve.wait_ge(S["pt_ready"], u - 1)
                if i == 0 and g == 0 and p >= 2:
                    dve.wait_ge(S["comb_done"], p - 1)
                if i == 0 and g and p:
                    dve.wait_ge(S[f"o_sent{g}"], 32 * p)
                o = out_tile(a)
                mk = mask2[:, :] if g == 2 else mask[:, :] if has_previous(g, i) else mask[:, P:2 * P]
                n = 2 * P if has_previous(g, i) else P
                for hh in range(2):
                    ins = dve.tensor_tensor_reduce(out=probs[:, u % 2, hh * 2 * P:hh * 2 * P + n],
                                                   in0=s_bank[hh][:, 0:n], in1=mk,
                                                   scale=1.0, scalar=-3e38, op0=ALU.add, op1=ALU.max,
                                                   accum_out=o[:, i, 2 * HD + hh:2 * HD + hh + 1])
                link(ins)
                dve.tensor_scalar(negmax[:, u % 2, :], o[:, i, 2 * HD:2 * HD + 2], -1.0, None,
                                  ALU.mult).then_inc(S["smax_done"], 1)

            def transposed(a, i):
                g = a % GROUPS
                u = NT * a + i
                dve.wait_ge(S["pt_ready"], u + 1)
                if u >= 2:
                    dve.wait_ge(S["o_ready"], u - 1)
                n = (4 if has_previous(g, i) else 2) * P
                dve.tensor_copy(pT[:, u % 2, 0:n], pt_bank[u % 2][:, 0:n]).then_inc(S["pt_out"], 1)

            def normalise(st, m):
                g = st % GROUPS
                dve.wait_ge(S["rstd_done"], 4 * st + m + 1)
                if st >= 2 and m == 0:
                    dve.wait_ge(S["s_ready"], NT * (st - 1))
                dst = (qT, kT)[m // 2][:, st % 2, :]
                col = (C_Q, C_K)[m // 2]
                dve.scalar_tensor_tensor(token_order(dst, g, m % 2), natural(qk_raw[:, m % 2, :], g),
                                         cols[:, col:col + 1], natural(rstd[:, m % 2, :], g),
                                         ALU.mult, ALU.mult).then_inc(S["qk_ready"], 1)

            def comb_small(p, part):
                ts = [o_own[p % 2], o_nat[0], o_nat[1]]
                mx = [t[:, :, 2 * HD:2 * HD + 2] for t in ts]
                dn = [t[:, :, 2 * HD + 2:2 * HD + 4] for t in ts]
                e = [cmb[:, 1 + g, :, :] for g in range(3)]
                top = cmb[:, 0, :, :]
                if part == 0:
                    dve.wait_ge(S["nat_in"], 32 * (p + 1))
                    if p:
                        dve.wait_ge(S["comb_done"], p)
                    dve.wait_ge(S["exp_done"], NT * (3 * p + 1))
                    link(dve.tensor_tensor(top, mx[0], mx[1], ALU.max))
                    link(dve.tensor_tensor(top, top, mx[2], ALU.max))
                    for g in range(3):
                        ins = dve.tensor_tensor(e[g], mx[g], top, ALU.subtract)
                    ins.then_inc(S["comb_d"], 1)
                else:
                    dve.wait_ge(S["comb_e"], p + 1)
                    t = cmb[:, 4, :, :]
                    link(dve.tensor_tensor(top, e[0], dn[0], ALU.mult))
                    for g in (1, 2):
                        link(dve.tensor_tensor(t, e[g], dn[g], ALU.mult))
                        link(dve.tensor_tensor(top, top, t, ALU.add))
                    link(dve.reciprocal(t, top))
                    for g in range(3):
                        ins = dve.tensor_tensor(e[g], e[g], t, ALU.mult)
                    ins.then_inc(S["comb_w"], 1)

            def gate_sum(k):
                dve.wait_ge(gate_in[k % 3], 16 * (k // 3 + 1))
                sc = small[:, SC + k:SC + k + 1]
                if k == 0:
                    ins = dve.tensor_scalar(gate_part, gate_w[:, 0, :], sc, None, ALU.mult)
                else:
                    dve.wait_ge(S["ada_used"], KB + k)
                    ins = dve.scalar_tensor_tensor(gate_part, gate_w[:, k % 3, :], sc, gate_part, ALU.mult, ALU.add)
                ins.then_inc(S["ada_used"], 1)

            for st in range(STAGES + 1):
                for slot in range(SLOTS):
                    m, k = divmod(slot, 8)
                    if k == 1 and 2 <= m <= 5 and st < STAGES:
                        normalise(st, m - 2)
                    if st == 0 and slot % 5 == 2 and slot // 5 < KB:
                        gate_sum(slot // 5)
                    if st == 1 and slot == 0:
                        dve.wait_ge(S["gate_bias"], 16)
                        for hh in range(2):
                            dve.wait_ge(S["gate_mm"], hh + 1)
                            gb = gate_bc[:, hh * HALF:(hh + 1) * HALF]
                            dve.tensor_tensor(gb, pt_bank[hh][:, :], gb, ALU.add).then_inc(S["gate_ready"], 1)
                    if not st:
                        continue
                    a = st - 1
                    i = slot // 5
                    if slot % 5 == 1 and i < NT:
                        maxima(a, i)
                    if slot % 5 == 2 and 1 <= i <= NT:
                        transposed(a, i - 1)
                    if st >= 4 and (st - 4) % 3 == 0:
                        if slot == 34:
                            comb_small((st - 4) // 3, 0)
                        if slot == 40:
                            comb_small((st - 4) // 3, 1)

            for e in range(8):
                p, tt = divmod(e, 2)
                half = slice(tt * HALF, (tt + 1) * HALF)
                if e == 2:
                    comb_small(PAIRS - 1, 0)
                    comb_small(PAIRS - 1, 1)
                dve.wait_ge(S["tr_ready"], e + 1)
                if e < 2:
                    dve.wait_ge(S["zs_ready"], e + 1)
                else:
                    wait_copied(dve, ("z", p, tt))
                if e >= 2:
                    dve.wait_ge(S["a_ready"], e - 1)
                dve.tensor_tensor(a32[:, e % 2, :], bank[2 + e % 2][:, :], z_silu[:, e % 2, :], ALU.mult).then_inc(S["a32_made"], 1)
                dve.wait_ge(S["a_hi_done"], e + 1)
                dve.tensor_tensor(a_lo[:, p, half], a32[:, e % 2, :], a_hi[:, p, half].bitcast(F32),
                                  ALU.subtract).then_inc(S["a_ready"], 1)
            def merged_low(k):
                half = slice((k % 2) * HALF, (k % 2 + 1) * HALF)
                dve.wait_ge(S["m_hi_done"], k + 1)
                dve.tensor_tensor(h_lo[:, k // 2, half], merged[:, k // 2, half], h_hi[:, k // 2, half].bitcast(F32),
                                  ALU.subtract).then_inc(S["m_ready"], 1)

            for j in range(KB):
                for tt in range(2):
                    s = SEG[("yA", j, tt)]
                    k = 2 * j + tt
                    half = slice(tt * HALF, (tt + 1) * HALF)
                    dve.wait_ge(S["pj_ready"], s + 1)
                    if k == 0:
                        dve.wait_ge(S["a_ready"], 8)
                        dve.wait_ge(S["ga_sigmoid"], 4)
                    dst = y32[:, k % 2, :]
                    ins = dve.tensor_tensor(dst, gate_tile("gA", j, tt), proj_bank[s % 2][:, :], ALU.mult)
                    ins.then_inc(pj_free[s % 2], 1)
                    wait_copied(dve, ("yA", j, tt))
                    dve.wait_ge(part_back[j], 16)
                    dve.tensor_tensor(merged[:, j, half], dst, merged[:, j, half], ALU.add).then_inc(S["merged_ready"], 1)
                    if j >= KB - 2:
                        for i in range(3):
                            merged_low(3 * (k - 12) + i)
            for k in range(12, 16):
                merged_low(k)
            for k in range(16):
                nn, t = divmod(k, NT)
                dve.wait_ge(S["out_full"], k + 1)
                if k >= NT:
                    dve.wait_ge(stored[k % NT], 16)
                dve.tensor_tensor(y_tile(k), bank[t][:, :], gate_bc[:, nn * HALF:(nn + 1) * HALF],
                                  ALU.mult).then_inc(S["out_scaled"], 1)
                if k >= NT and k % 2:
                    dve.wait_ge(S["out_scaled"], k + 1)
                    dve.wait_ge(x_again[k % NT], 16 * (k // NT + 1))
                    dve.tensor_tensor(y_tile(k), y_tile(k), x_tile(k), ALU.add).then_inc(out_made[1], 1)


_INS = ["x", "c", "w_ada", "b_ada", "norm_w", "w_in", "b_gate", "q_norm_w", "k_norm_w", "w_attn_proj",
        "conv_w", "conv_b", "conv_ln_w", "conv_ln_b", "w_conv_proj", "w_out"]


def kernel(**inputs):
    import numpy as _np
    import concourse.bacc as _bacc
    from concourse import mybir as _mybir
    from concourse.bass_utils import run_bass_kernel_spmd as _run

    nc = _bacc.Bacc("TRN2", target_bir_lowering=False, num_devices=1)
    arrays, args = {}, {}
    for name in _INS:
        a = _np.ascontiguousarray(inputs[name])
        arrays[f"in_{name}_dram"] = a
        args[name] = nc.dram_tensor(f"in_{name}_dram", a.shape, _mybir.dt.from_np(a.dtype), kind="ExternalInput").ap()
    args["out"] = nc.dram_tensor("out_0_dram", (1, 1024, 1024), _mybir.dt.float32, kind="ExternalOutput").ap()
    build(nc, **args)
    r = _run(nc, [arrays], core_ids=[0])
    return r.results[0]["out_0_dram"]
```

```python
from contextlib import ExitStack

import concourse.bass as bass
from concourse import mybir

P = 128
T = 1024
D = 1024
KB = D // P
NT = T // P
HALF = 512
CW = 512
CB = CW // P
TAPS = 31
PAD = TAPS - 1
HD = 64
PAIRS = 4
GROUPS = 3
DILATION = (1, 4, 16)
OW = 2 * HD + 4
EPS = 1e-6
MASKED = -1e30

Q0, K0, V0, ZA0, UA0, UB0, ZC0, GA0, GB0 = 0, 1536, 3072, 4608, 5120, 5632, 6144, 6656, 7680

F32 = mybir.dt.float32
F32R = mybir.dt.float32r
ALU = mybir.AluOpType
ACT = mybir.ActivationFunctionType

STAGES = PAIRS * GROUPS
SLOTS = 48


def blocks():
    out = []
    for c in range(CB):
        out += [("convb", c), ("conva", c), ("convz", c)]
    out += [("gB", j) for j in range(6)] + [("pB", i) for i in range(3)] + [("gB", 6), ("gB", 7), ("pB", 3)]
    for st in range(STAGES):
        out += [("q", st), ("k", st), ("v", st)]
    out += [("gA", 0), ("gA", 1)] + [("z", p) for p in range(PAIRS)] + [("pA", 0)]
    for i in range(1, KB // 2):
        out += [("gA", 2 * i), ("gA", 2 * i + 1), ("pA", i)]
    out += [("out", k) for k in range(8)]
    return out


BLOCKS = blocks()
NO = {b: n for n, b in enumerate(BLOCKS)}


def segments():
    seg, last = {}, {}
    for tt in range(2):
        for n in range(3):
            last[n] = seg[(*BLOCKS[n], tt)] = len(seg)
    for n, (kind, w) in enumerate(BLOCKS):
        if n < 3:
            continue
        if kind == "out":
            continue
        parts = [(kind, w)] if kind not in ("pA", "pB") else [("y" + kind[1], 2 * w), ("y" + kind[1], 2 * w + 1)]
        for part in parts:
            for tt in range(2):
                last[n] = seg[(*part, tt)] = len(seg)
    return seg, last


SEG, LAST_SEG = segments()
ADA = 6
RAW, WR = 2, 3
GB_BEFORE = 3
POOL_TAPS = 8


def conv_halves(c):
    halves = [(kind, c, tt) for kind in ("convb", "conva", "convz") for tt in range(2)]
    return sorted(halves, key=lambda key: SEG[key])


def conv_schedule():
    keys = [key for c in range(CB) for key in conv_halves(c)] + [("gB", j, tt) for j in range(GB_BEFORE) for tt in range(2)]
    steps = []
    for h, (kind, w, tt) in enumerate(keys):
        early = {0: 2, 3: 3, 4: 4}
        weights = early.get(h) if h < 6 else NO[(kind, w)] + 2 if tt == 0 else None
        c, at = divmod(h - 4, 6)
        spread = [[], [0, 1, 2, 3], [4], [5], [6], [7]] if c == 0 else [[0, 1], [2, 3], [4], [5], [6], [7]]
        steps.append((kind, w, tt, weights, [(c, i) for i in spread[at]] if 0 <= c < CB else []))
    return steps


def build(nc, x, c, w_ada, b_ada, norm_w, w_in, b_gate, q_norm_w, k_norm_w, w_attn_proj,
          conv_w, conv_b, conv_ln_w, conv_ln_b, w_conv_proj, w_out, out):
    ctx = ExitStack()
    with ctx:
        def sb(name, shape, dt=F32, stack=ctx):
            return stack.enter_context(nc.sbuf_tensor(name, shape, dt))

        def sem(name):
            return ctx.enter_context(nc.semaphore(name))

        bank = [ctx.enter_context(nc.psum_tensor(f"bank{i}", [P, HALF], F32)) for i in range(8)]
        proj_bank, aux, s_bank, pt_bank, o_bank = bank[0:2], bank[2], bank[3:5], bank[5:7], bank[7]

        o_dram = [nc.dram_tensor(f"o_dram{g}", [PAIRS, T, OW], F32, kind="Internal") for g in (1, 2)]
        part_dram = nc.dram_tensor("part_dram", [KB, P, T], F32, kind="Internal")

        h_hi = sb("h_hi", [P, KB, T], F32R)
        h_lo = sb("h_lo", [P, KB, T], F32R)
        raw = sb("raw", [P, RAW, 1024])
        w_hi = sb("w_hi", [P, WR, 1024], F32R)
        w_lo = sb("w_lo", [P, WR, 1024], F32R)
        attn = sb("attn", [P, NT, CW])
        sg = sb("sg", [P, 4, HALF])
        gate_bc = sb("gate_bc", [P, D])
        ident = sb("ident", [P, P])
        ones_w = sb("ones_w", [P, P])
        mean_w = sb("mean_w", [P, P])
        head_w = sb("head_w", [P, P])
        mean_wr = sb("mean_wr", [P, P], F32R)
        head_wr = sb("head_wr", [P, P], F32R)
        mask = sb("mask", [P, 2 * P])
        mask2 = sb("mask2", [P, P])
        cols = sb("cols", [P, 72])
        conv_col = sb("conv_col", [P, CB, TAPS])
        eps = sb("eps", [P, 1])
        small = sb("small", [P, 40])
        cmb = sb("cmb", [P, 5, NT, 2])

        with ExitStack() as s:
            xt = sb("xt", [P, NT, D], stack=s)
            ada_w = sb("ada_w", [P, ADA, D], stack=s)
            ada_part = sb("ada_part", [P, 2 * D], stack=s)
            junk = sb("junk", [P, D], stack=s)
            h32 = sb("h32", [P, 2, HALF], stack=s)
            rows = sb("rows", [72, P], stack=s)
            conv_rows = sb("conv_rows", [TAPS, CW], stack=s)
        with ExitStack() as s:
            glu = sb("glu", [P, 2, PAD + T], stack=s)
            acc_b = sb("acc_b", [P, T], stack=s)
            cv = sb("cv", [P, CB, T], stack=s)
            zc = sb("zc", [P, CB, T], stack=s)
            with ExitStack() as s2:
                tap_sum = sb("tap_sum", [P, 2, T], stack=s2)
                tap = sb("tap", [P, 2, T], stack=s2)
            c_hi = sb("c_hi", [P, CB, T], F32R, stack=s)
            c_lo = sb("c_lo", [P, CB, T], F32R, stack=s)
        with ExitStack() as s:
            qT = sb("qT", [P, 2, T], stack=s)
            kT = sb("kT", [P, 2, T], stack=s)
            vT = sb("vT", [P, T], stack=s)
            v = sb("v", [P, NT, P], stack=s)
            qk_raw = sb("qk_raw", [P, 2, HALF], stack=s)
            rstd = sb("rstd", [P, 2, HALF], stack=s)
            sq_hi = sb("sq_hi", [P, 2, HALF], F32R, stack=s)
            sq_lo = sb("sq_lo", [P, 2, HALF], F32R, stack=s)
            probs = sb("probs", [P, 2, 2 * 2 * P], stack=s)
            pT = sb("pT", [P, 2, 4 * P], stack=s)
            o_own = [sb(f"o_own{i}", [P, NT, OW], stack=s) for i in range(4)]
            o_nat = [sb(f"o_nat{i}", [P, NT, OW], stack=s) for i in range(2)]
            negmax = sb("negmax", [P, 2, 2], stack=s)
        with ExitStack() as s:
            z_silu = sb("z_silu", [P, 2, HALF], stack=s)
            a32 = sb("a32", [P, 2, HALF], stack=s)
            a_hi = sb("a_hi", [P, CB, T], F32R, stack=s)
            a_lo = sb("a_lo", [P, CB, T], F32R, stack=s)
            merged = sb("merged", [P, KB, T], stack=s)
        with ExitStack() as s:
            y_out = sb("y_out", [P, NT, HALF], stack=s)
        y32 = a32

        names = """rows_in c_in consts c_col cols_ready cols_copied sc_ready ada_used ada_cols mod_ready
            xsq rstd_x x_scaled xt_ready h_copied h_ready w_hi_done w_split
            pj_ready glu_ready tap_made tap_added conv_part conv_done conv_hi conv_lo mean_ready centered
            ln_sq_hi sq_ready var_ready ln_r ln_scaled ln_silu ln_z c_hi_done c_ready
            gate_bias gate_mm gate_ready sq_hi_done sq_lo_done ss_ready ln_done rstd_done qk_ready vtr_ready v_ready
            s_ready smax_done exp_done pt_ready pt_out o_ready o_out o_sent1 o_sent2 nat_in
            comb_d comb_e comb_w comb_done tr_ready zs_ready a32_made a_hi_done a_ready ga_sigmoid
            merged_ready m_hi_done m_ready out_ready out_full out_scaled
            dve_chain act_chain pool_chain""".split()
        S = {n: sem(n) for n in names}
        pj_free = [sem("pj_free0"), sem("pj_free1")]
        x_in = [sem(f"x_in{i}") for i in range(NT // 2)]
        ada_in = [sem(f"ada_in{i}") for i in range(ADA)]
        gate_in = [sem(f"gate_in{i}") for i in range(3)]
        raw_in = [sem(f"raw_in{i}") for i in range(RAW)]
        part_out = [sem(f"part_out{i}") for i in range(4)]
        part_back = [sem(f"part_back{i}") for i in range(KB)]
        x_again = [sem(f"x_again{i}") for i in range(NT)]
        out_made = [sem("out_made0"), sem("out_made1")]
        stored = [sem(f"stored{i}") for i in range(NT)]

        w_in3 = w_in[0].rearrange("(k p) n -> p k n", p=P)
        proj3 = {"pA": w_attn_proj[0].rearrange("(k p) n -> p k n", p=P),
                 "pB": w_conv_proj[0].rearrange("(k p) n -> p k n", p=P)}
        wout3 = w_out[0].rearrange("(k p) n -> p k n", p=P)
        x3 = x[0].rearrange("(i p) d -> p i d", p=P)
        out3 = out[0].rearrange("(i p) d -> p i d", p=P)
        base = {"convb": UB0, "conva": UA0, "convz": ZC0, "gA": GA0, "gB": GB0, "z": ZA0}

        def block_source(n):
            kind, w = BLOCKS[n]
            r = raw[:, n % RAW, :]
            if kind == "out":
                nn, kk = divmod(w, 4)
                return (r.rearrange("p (k n) -> p k n", k=2),
                        wout3[:, 2 * kk:2 * kk + 2, nn * HALF:(nn + 1) * HALF])
            if kind in ("pA", "pB"):
                return r.rearrange("p (k n) -> p k n", k=CB), proj3[kind][:, :, 2 * P * w:2 * P * (w + 1)]
            if kind in ("q", "k", "v"):
                p, g = divmod(w, GROUPS)
                col = {"q": Q0, "k": K0, "v": V0}[kind] + g * CW + p * P
            else:
                col = base[kind] + w * P
            return r.rearrange("p (k n) -> p k n", k=KB), w_in3[:, :, col:col + P]

        def token_order(ap, g, tt):
            d = DILATION[g]
            n = HALF // d
            return ap.rearrange("p (r l) -> p l r", r=d)[:, n * tt:n * (tt + 1), :]

        def wait_copied(eng, key):
            eng.wait_ge(pj_free[SEG[key] % 2], SEG[key] // 2 + 1)

        def natural(ap, g):
            return ap.rearrange("p (l r) -> p l r", r=DILATION[g])

        def has_previous(g, i):
            return i >= 1 if g == 0 else i % 2 == 1 if g == 1 else False

        def out_tile(a):
            p, g = divmod(a, GROUPS)
            return o_own[p % 2] if g == 0 else o_own[1 + g]

        C_C, C_BADA, C_NORM, C_BG, C_CB, C_LW, C_LB, C_Q, C_K = 0, 8, 32, 40, 56, 60, 64, 68, 69
        NROWS = 70
        SC, SHIFT, SCALE_, SS, RS = 0, 8, 16, 24, 32
        gate_w = attn[:, 0:6, :].rearrange("p (a b) n -> p a (b n)", a=3)
        gate_part = attn[:, 6:8, :].rearrange("p b n -> p (b n)")

        def gate_tile(kind, j, tt):
            if kind == "gB" and 2 <= j < 6:
                return attn[:, 2 * (j - 2) + tt, :]
            return sg[:, 2 * (j % 2) + tt, :]

        def square_tile(cc):
            return (glu[:, 0, :], acc_b[:, :])[cc // 2][:, (cc % 2) * HALF:(cc % 2 + 1) * HALF]

        def y_tile(k):
            return y_out[:, k % NT, :]

        def x_tile(k):
            return attn[:, k % NT, :]

        def attn_transposes(pe, e):
            p, tt = divmod(e, 2)
            pe.wait_ge(S["comb_done"], p + 1)
            if e >= 2:
                pe.wait_ge(S["a32_made"], e - 1)
            elif e == 1:
                pe.wait_ge(S["smax_done"], NT * STAGES)
            else:
                pe.wait_ge(S["v_ready"], 2 * STAGES)
            for i in range(4):
                ins = pe.transpose(bank[2 + e % 2][:, i * P:(i + 1) * P],
                                   attn[:, 4 * tt + i, p * P:(p + 1) * P], ident[:, :])
            ins.then_inc(S["tr_ready"], 1)

        def a_high(e, act):
            p, tt = divmod(e, 2)
            act.wait_ge(S["a32_made"], e + 1)
            act.activation(a_hi[:, p, tt * HALF:(tt + 1) * HALF], a32[:, e % 2, :], ACT.Copy).then_inc(S["a_hi_done"], 1)

        block = ctx.enter_context(nc.Block())

        @block.sync
        def _(sp):
            with nc.allow_non_contiguous_dma(reason="weight columns"):
                def load_x(i):
                    sp.dma_start(xt[:, 2 * i:2 * i + 2, :], x3[:, 2 * i:2 * i + 2, :]).then_inc(x_in[i], 16)

                def load_block(n):
                    sp.dma_start(*block_source(n)).then_inc(raw_in[n % RAW], 16)

                sp.dma_start(rows[C_C:C_C + 8, :], c[0].rearrange("(k p) -> k p", p=P)).then_inc(S["c_in"], 16)
                load_x(0)
                load_x(1)
                wa = w_ada[0].rearrange("(k p) n -> p k n", p=P)
                for n in range(2 * KB):
                    half, k = divmod(n, KB)
                    if n >= ADA:
                        sp.wait_ge(S["ada_used"], n - ADA + 1)
                    sp.dma_start(ada_w[:, n % ADA, :].rearrange("p (s n) -> p s n", s=2),
                                 wa[:, k, 0:2 * D].rearrange("p (s h n) -> p s h n", s=2, h=2)[:, :, half, :]
                                 ).then_inc(ada_in[n % ADA], 16)
                    if n in (4, 7):
                        load_block(n // 7)
                    if n == KB + 3:
                        load_x(2)
                        load_x(3)
                gate_loads = {NO[("q", 0)] + 1: (0, 1, 2), NO[("q", 0)] + 2: (3, 4),
                              NO[("q", 0)] + 3: (5, 6), NO[("q", 0)] + 4: (7,)}
                natural_read = {NO[("q", 3 * p + 4)] + 4: p for p in range(PAIRS - 1)}
                natural_read[NO[("z", 0)] + 4] = PAIRS - 1
                for n in range(RAW, len(BLOCKS)):
                    sp.wait_ge(S["w_split"], n - RAW + 1)
                    load_block(n)
                    for k in gate_loads.get(n, ()):
                        if k == 0:
                            wait_copied(sp, ("yB", 5, 0))
                            wait_copied(sp, ("yB", 5, 1))
                        if k >= 3:
                            sp.wait_ge(S["ada_used"], 2 * KB + k - 2)
                        sp.dma_start(gate_w[:, k % 3, :], wa[:, k, 2 * D:3 * D]).then_inc(gate_in[k % 3], 16)
                    if n in natural_read:
                        p = natural_read[n]
                        if p:
                            sp.wait_ge(S["comb_done"], p)
                        sp.wait_ge(S["o_sent1"], 32 * (p + 1))
                        sp.wait_ge(S["o_sent2"], 32 * (p + 1))
                        for g in range(2):
                            sp.dma_start(o_nat[g][:, :, :],
                                         o_dram[g].ap()[p].rearrange("(i p) w -> p i w", p=P)).then_inc(S["nat_in"], 16)
                    kind, w = BLOCKS[n - 1]
                    if kind == "pA":
                        if w == 0:
                            for q in part_out:
                                sp.wait_ge(q, 32)
                            sp.wait_ge(S["comb_done"], PAIRS)
                        for j in (2 * w, 2 * w + 1):
                            sp.dma_start(merged[:, j, :], part_dram.ap()[j]).then_inc(part_back[j], 16)
                for k in range(16):
                    sp.wait_ge(out_made[k % 2], k // 2 + 1)
                    nn, t = divmod(k, NT)
                    sp.dma_start(out3[:, t, nn * HALF:(nn + 1) * HALF], y_tile(k)).then_inc(stored[k % NT], 16)
                for q in stored:
                    sp.wait_ge(q, 32)

        @block.gpsimd
        def _(pool):
            chain = [0]

            def link(ins):
                chain[0] += 1
                ins.then_inc(S["pool_chain"], 1)
                pool.wait_ge(S["pool_chain"], chain[0])

            link(pool.memset(ident[:, :], 0.0))
            link(pool.memset(mean_w[:, :], 1.0 / CW))
            link(pool.memset(ones_w[:, :], 1.0))
            link(pool.memset(eps[:, :], EPS))
            link(pool.memset(head_w[:, :], 0.0))
            link(pool.memset(mask[:, :], 0.0))
            link(pool.memset(mask2[:, :], 0.0))
            link(pool.affine_select(out=ident[:, :], in_=ident[:, :], compare_op=ALU.not_equal, fill=1.0,
                                    base=0, pattern=[[-1, P]], channel_multiplier=1))
            link(pool.memset(head_w[0:HD, 0:HD], 1.0 / HD))
            link(pool.memset(head_w[HD:P, HD:P], 1.0 / HD))
            link(pool.affine_select(out=mask[:, 0:P], in_=mask[:, 0:P], compare_op=ALU.is_ge, fill=MASKED,
                                    base=0, pattern=[[1, P]], channel_multiplier=-1))
            link(pool.affine_select(out=mask[:, P:2 * P], in_=mask[:, P:2 * P], compare_op=ALU.is_ge, fill=MASKED,
                                    base=0, pattern=[[-1, P]], channel_multiplier=1))
            link(pool.affine_select(out=mask2[:, :], in_=mask2[:, :], compare_op=ALU.is_ge, fill=MASKED,
                                    base=0, pattern=[[-1, P]], channel_multiplier=1))
            link(pool.tensor_copy(head_wr[:, :], head_w[:, :]))
            link(pool.tensor_copy(mean_wr[:, :], mean_w[:, :]))
            pool.memset(mask2[HD:P, 0:HD], MASKED).then_inc(S["consts"], 1)

            def split(n):
                pool.wait_ge(S["w_hi_done"], n + 1)
                pool.tensor_tensor(w_lo[:, n % WR, :], raw[:, n % RAW, :], w_hi[:, n % WR, :].bitcast(F32),
                                   ALU.subtract).then_inc(S["w_split"], 1)

            def combine(p, step):
                tiles = [o_own[p % 2], o_nat[0], o_nat[1]]
                view = [t[:, :, 0:2 * HD].rearrange("p i (h d) -> p i h d", h=2) for t in tiles]
                if step < 3:
                    pool.wait_ge(S["comb_w"], p + 1)
                    w = cmb[:, 1 + step, :, :].unsqueeze(3).to_broadcast([P, NT, 2, HD])
                    link(pool.tensor_tensor(view[step], view[step], w, ALU.mult))
                elif step == 3:
                    link(pool.tensor_tensor(view[0], view[0], view[1], ALU.add))
                else:
                    pool.tensor_tensor(attn[:, :, p * P:(p + 1) * P].rearrange("p i (h d) -> p i h d", h=2),
                                       view[0], view[2], ALU.add).then_inc(S["comb_done"], 1)

            split(0)
            split(1)
            pool_first = NO[("gB", GB_BEFORE - 1)] + 3
            for kind, c, tt, weights, taps in conv_schedule():
                if kind == "conva":
                    if c >= 2:
                        pool.wait_ge(S["conv_done"], c - 1)
                    elif tt == 0:
                        if c == 0:
                            pool.wait_ge(S["h_ready"], 16)
                        pool.memset(glu[:, c, 0:PAD], 0.0)
                    wait_copied(pool, ("convb", c, tt))
                    wait_copied(pool, ("conva", c, tt))
                    pool.tensor_tensor(glu[:, c % 2, PAD + tt * HALF:PAD + (tt + 1) * HALF],
                                       sg[:, tt, :], sg[:, 2 + tt, :], ALU.mult).then_inc(S["glu_ready"], 1)
                if weights:
                    split(weights)
                for tc, i in taps:
                    if i == 0:
                        continue
                    t = (POOL_TAPS - 1) * tc + i - 1
                    pool.wait_ge(S["tap_made"], POOL_TAPS * tc + i + 1)
                    if t:
                        pool.wait_ge(S["tap_added"], t)
                    pool.tensor_tensor(tap_sum[:, tc % 2, :], tap_sum[:, tc % 2, :], tap[:, t % 2, :],
                                       ALU.add).then_inc(S["tap_added"], 1)
            for n in range(pool_first, NO[("pB", 2)] + 1):
                split(n)
            combine_after = {NO[("q", 3 * p + 4)] + 5 + i: [(p, i)] for p in range(PAIRS - 1) for i in range(5)}
            combine_after[NO[("z", 0)] + 4] = [(PAIRS - 1, i) for i in range(5)]
            def square_low(st, m):
                pool.wait_ge(S["sq_hi_done"], 4 * st + m + 1)
                pool.tensor_tensor(sq_lo[:, m % 2, :], rstd[:, m % 2, :], sq_hi[:, m % 2, :].bitcast(F32),
                                   ALU.subtract).then_inc(S["sq_lo_done"], 1)

            for n in range(NO[("pB", 2)] + 1, len(BLOCKS) - 1):
                kind, st = BLOCKS[n - 2]
                if kind in ("q", "k"):
                    square_low(st, 2 * "qk".index(kind))
                split(n)
                if kind in ("q", "k"):
                    square_low(st, 2 * "qk".index(kind) + 1)
                for step in combine_after.get(n, ()):
                    combine(*step)
            for k in range(16):
                if k == NT:
                    split(len(BLOCKS) - 1)
                if k >= NT and k % 2:
                    continue
                pool.wait_ge(x_again[k % NT], 16 * (k // NT + 1))
                pool.wait_ge(S["out_scaled"], k + 1)
                pool.tensor_tensor(y_tile(k), y_tile(k), x_tile(k), ALU.add).then_inc(out_made[k % 2], 1)

        @block.tensor
        def _(pe):
            w8 = [[w[:, i, :].rearrange("p (k n) -> p k n", k=KB) for i in range(WR)] for w in (w_hi, w_lo)]
            w4 = [[w[:, i, :].rearrange("p (k n) -> p k n", k=CB) for i in range(WR)] for w in (w_hi, w_lo)]
            w2 = [[w[:, i, :].rearrange("p (k n) -> p k n", k=2) for i in range(WR)] for w in (w_hi, w_lo)]

            def three(o, lh, ll, rh, rl, first, last):
                pe.matmul(o, lh, rh, start=first, stop=False)
                pe.matmul(o, lh, rl, start=False, stop=False)
                return pe.matmul(o, ll, rh, start=False, stop=last)

            def project(kind, w, tt, slot=None, before=None, ks=range(KB)):
                n, s = NO[(kind, w)], SEG[(kind, w, tt)]
                pe.wait_ge(S["w_split"], n + 1)
                if s >= 2:
                    pe.wait_ge(pj_free[s % 2], s // 2)
                for k in ks:
                    if before:
                        before(k)
                    cols_ = slice(tt * HALF, (tt + 1) * HALF)
                    ins = three(proj_bank[s % 2][:, :], w8[0][n % WR][:, k, :], w8[1][n % WR][:, k, :],
                                h_hi[:, k, cols_], h_lo[:, k, cols_], k == 0, k == KB - 1)
                    if k == KB - 1:
                        ins.then_inc(S["pj_ready"], 1)
                    if slot:
                        slot(k)

            def branch_out(kind, j, tt, hi, lo):
                n, s = NO[("p" + kind, j // 2)], SEG[("y" + kind, j, tt)]
                pe.wait_ge(S["w_split"], n + 1)
                pe.wait_ge(pj_free[s % 2], s // 2)
                for k in range(CB):
                    if kind == "A" and j == 0:
                        pe.wait_ge(S["a_ready"], 2 * k + tt + 1)
                    wc, tc = slice((j % 2) * P, (j % 2 + 1) * P), slice(tt * HALF, (tt + 1) * HALF)
                    ins = three(proj_bank[s % 2][:, :], w4[0][n % WR][:, k, wc], w4[1][n % WR][:, k, wc],
                                hi[:, k, tc], lo[:, k, tc], k == 0, k == CB - 1)
                ins.then_inc(S["pj_ready"], 1)

            pe.wait_ge(S["consts"], 1)
            pe.wait_ge(S["c_in"], 16)
            pe.transpose(bank[1][:, 0:KB], rows[C_C:C_C + KB, :], ident[0:KB, 0:KB]).then_inc(S["c_col"], 1)
            pe.wait_ge(S["rows_in"], 16 * 9)
            pe.transpose(bank[0][:, 0:NROWS], rows[0:NROWS, :], ident[0:NROWS, 0:NROWS])
            for cc in range(CB):
                ins = pe.transpose(bank[0][:, 128 + 32 * cc:128 + 32 * cc + TAPS], conv_rows[:, cc * P:(cc + 1) * P],
                                   ident[0:TAPS, 0:TAPS])
            ins.then_inc(S["cols_ready"], 1)

            def x_transposes(m):
                tt, k = divmod(m, KB)
                pe.wait_ge(S["x_scaled"], 4 * tt + 4)
                if m >= 5:
                    pe.wait_ge(S["h_copied"], m - 4)
                for i in range(4):
                    ins = pe.transpose(bank[2 + m % 5][:, i * P:(i + 1) * P],
                                       xt[:, 4 * tt + i, k * P:(k + 1) * P], ident[:, :])
                ins.then_inc(S["xt_ready"], 1)

            def ada_sums(half):
                pe.wait_ge(S["ada_used"], KB * (half + 1))
                for q in range(KB):
                    col = KB * (q // 4) + 4 * half + q % 4
                    ins = pe.matmul(bank[7][:, col:col + 1], ada_part[:, half * D + q * P:half * D + (q + 1) * P],
                                    ones_w[:, 0:1], start=True, stop=True)
                ins.then_inc(S["ada_cols"], 1)

            for m in range(2):
                x_transposes(m)
            ada_sums(0)
            for m in range(2, 5):
                x_transposes(m)
            pe.wait_ge(S["mod_ready"], 1)

            def h_there(k):
                pe.wait_ge(S["h_ready"], k + 1)

            project(*conv_halves(0)[0], before=h_there, ks=range(4))
            for m in range(5, KB):
                x_transposes(m)
            project(*conv_halves(0)[1], before=h_there, ks=range(4))
            ada_sums(1)
            for cc in range(CB):
                for h_no, key in enumerate(conv_halves(cc)):
                    def before(k):
                        if cc == 0 and h_no in (0, 3):
                            pe.wait_ge(S["h_ready"], KB * key[2] + k + 1)
                        if cc == 0 and h_no == 1 and k == KB - 1:
                            for m in range(8, 13):
                                x_transposes(m)
                        if cc == 0 and h_no == 2 and k >= 5:
                            x_transposes(8 + k)
                    project(*key, before=before, ks=range(4, KB) if cc == 0 and h_no < 2 else range(KB))
            for j in range(GB_BEFORE):
                for tt in range(2):
                    project("gB", j, tt)
            def channel_mean(o, cc, tt):
                half = slice(tt * HALF, (tt + 1) * HALF)
                pe.matmul(o, mean_wr[:, :], c_hi[:, cc, half], start=(cc == 0), stop=False)
                return pe.matmul(o, mean_wr[:, :], c_lo[:, cc, half], start=False, stop=(cc == CB - 1))

            for cc in range(CB):
                pe.wait_ge(S["conv_lo"], cc + 1)
                for tt in range(2):
                    ins = channel_mean(bank[2 + 2 * tt][:, :], cc, tt)
                    if cc == CB - 1:
                        ins.then_inc(S["mean_ready"], 1)

            def variance(tt, cc):
                pe.wait_ge(S["sq_ready"], CB * tt + cc + 1)
                channel_mean(bank[3 + 2 * tt][:, :], cc, tt).then_inc(S["var_ready"], 1)

            for j in range(GB_BEFORE, 6):
                for tt in range(2):
                    at = {4 + i: i for i in range(CB)} if tt == 0 else {2 * i + 1: i for i in range(CB)}
                    project("gB", j, tt, slot=lambda k: variance(tt, at[k]) if j == GB_BEFORE and k in at else None)
            for i in range(KB // 2):
                if i == 3:
                    for j in (6, 7):
                        for tt in range(2):
                            project("gB", j, tt)
                for j in (2 * i, 2 * i + 1):
                    for tt in range(2):
                        if i == 0 and j == 0:
                            pe.wait_ge(S["c_ready"], CB * (tt + 1))
                        branch_out("B", j, tt, c_hi, c_lo)

            def attend(st, slot):
                a = st - 1
                g = a % GROUPS
                if slot in (3, 6):
                    hh = slot // 6
                    wait_copied(pe, ("v", a, 0))
                    wait_copied(pe, ("v", a, 1))
                    if hh:
                        pe.wait_ge(S["v_ready"], 2 * a + 1)
                    else:
                        pe.wait_ge(S["ln_done"], 4 * st if st < STAGES else 4 * STAGES)
                    for i in range(4):
                        t = 4 * hh + i
                        ins = pe.transpose(aux[:, i * P:(i + 1) * P], vT[:, t * P:(t + 1) * P], ident[:, :])
                    ins.then_inc(S["vtr_ready"], 1)
                if slot % 5 == 0 and slot // 5 < NT:
                    i = slot // 5
                    u = NT * a + i
                    if i == 0:
                        pe.wait_ge(S["qk_ready"], 4 * (a + 1))
                    if u:
                        pe.wait_ge(S["smax_done"], u)
                    first = i - 1 if has_previous(g, i) else i
                    n = (i + 1 - first) * P
                    for hh in range(2):
                        hp = slice(hh * HD, (hh + 1) * HD)
                        ins = pe.matmul(s_bank[hh][:, 0:n], qT[hp, a % 2, i * P:(i + 1) * P],
                                        kT[hp, a % 2, first * P:(i + 1) * P], start=True, stop=True)
                    ins.then_inc(S["s_ready"], 1)
                if slot % 5 == 2 and 1 <= slot // 5 <= NT:
                    i = slot // 5 - 1
                    u = NT * a + i
                    pe.wait_ge(S["exp_done"], u + 1)
                    if u == 0:
                        pe.wait_ge(S["gate_ready"], 2)
                    if u >= 2:
                        pe.wait_ge(S["pt_out"], u - 1)
                    chunks = 2 if has_previous(g, i) else 1
                    for hh in range(2):
                        for b in range(chunks):
                            ins = pe.transpose(pt_bank[u % 2][:, (chunks * hh + b) * P:(chunks * hh + b + 1) * P],
                                               probs[:, u % 2, (2 * hh + b) * P:(2 * hh + b + 1) * P], ident[:, :])
                    ins.then_inc(S["pt_ready"], 1)
                if slot % 5 == 4 and 1 <= slot // 5 <= NT:
                    i = slot // 5 - 1
                    u = NT * a + i
                    pe.wait_ge(S["pt_out"], u + 1)
                    if i == 0:
                        pe.wait_ge(S["v_ready"], 2 * (a + 1))
                    if u:
                        pe.wait_ge(S["o_out"], u)
                    chunks = 2 if has_previous(g, i) else 1
                    for hh in range(2):
                        for b in range(chunks):
                            ins = pe.matmul(o_bank[:, hh * HD:(hh + 1) * HD],
                                            pT[:, u % 2, (chunks * hh + b) * P:(chunks * hh + b + 1) * P],
                                            v[:, i - chunks + 1 + b, hh * HD:(hh + 1) * HD],
                                            start=(b == 0), stop=(b == chunks - 1))
                    ins.then_inc(S["o_ready"], 1)

            def head_mean(st, m):
                pe.wait_ge(S["sq_lo_done"], 4 * st + m + 1)
                if m:
                    pe.wait_ge(S["ln_done"], 4 * st + m)
                elif st:
                    pe.wait_ge(S["v_ready"], 2 * st)
                pe.matmul(aux[:, :], head_wr[:, :], sq_hi[:, m % 2, :], start=True, stop=False)
                pe.matmul(aux[:, :], head_wr[:, :], sq_lo[:, m % 2, :], start=False, stop=True).then_inc(S["ss_ready"], 1)

            for st in range(STAGES + 1):
                if st < STAGES:
                    halves = [(kind, st, tt) for kind in "qkv" for tt in range(2)]
                else:
                    halves = [(kind, j, tt) for kind, j in (("gA", 0), ("gA", 1), ("z", 0)) for tt in range(2)]
                for m in range(6):
                    def slot(k):
                        if st:
                            attend(st, 8 * m + k)
                        if k == 5 and 1 <= m <= 4 and st < STAGES:
                            head_mean(st, m - 1)
                        if st == 0 and m == 5 and k == 6:
                            pe.wait_ge(S["ada_used"], 3 * KB)
                            for hh in range(2):
                                pe.matmul(pt_bank[hh][:, :], ones_w[:, :], gate_part[:, hh * HALF:(hh + 1) * HALF],
                                          start=True, stop=True).then_inc(S["gate_mm"], 1)
                    project(*halves[m], slot)

            for p in range(1, PAIRS):
                for tt in range(2):
                    project("z", p, tt)
                    attn_transposes(pe, 2 * p + tt - 2)
            for e in (6, 7):
                attn_transposes(pe, e)
            for i in range(KB // 2):
                if i:
                    for j in (2 * i, 2 * i + 1):
                        for tt in range(2):
                            project("gA", j, tt)
                for j in (2 * i, 2 * i + 1):
                    for tt in range(2):
                        branch_out("A", j, tt, a_hi, a_lo)
            for nn in range(2):
                for kk in range(4):
                    n = NO[("out", 4 * nn + kk)]
                    pe.wait_ge(S["w_split"], n + 1)
                    steps = ([(kb2, t) for t in range(NT) for kb2 in range(2)] if kk == 3 else
                             [(kb2, (t + 2) % NT) for kb2 in range(2) for t in range(NT)] if (nn, kk) == (0, 0) else
                             [(kb2, t) for kb2 in range(2) for t in range(NT)])
                    for kb2, t in steps:
                        k = 2 * kk + kb2
                        if nn == 0:
                            pe.wait_ge(S["m_ready"], 2 * k + 2)
                        if k == 0 and nn == 1:
                            pe.wait_ge(S["out_scaled"], t + 1)
                        if k == 0 and nn == 0 and t < 2:
                            wait_copied(pe, ("yA", KB - 1, t))
                        tc = slice(t * P, (t + 1) * P)
                        o = bank[t][:, :]
                        pe.matmul(o, h_hi[:, k, tc], w2[0][n % WR][:, kb2, :], start=(k == 0), stop=False)
                        pe.matmul(o, h_hi[:, k, tc], w2[1][n % WR][:, kb2, :], start=False, stop=False)
                        ins = pe.matmul(o, h_lo[:, k, tc], w2[0][n % WR][:, kb2, :], start=False, stop=(k == KB - 1))
                        if k == KB - 1:
                            ins.then_inc(S["out_full"], 1)
                        elif (kb2, t) == steps[-1]:
                            ins.then_inc(S["out_ready"], 1)

        @block.scalar
        def _(act):
            chain = [0]

            def link(ins):
                chain[0] += 1
                ins.then_inc(S["act_chain"], 1)
                act.wait_ge(S["act_chain"], chain[0])

            def rs(r, n, ap):
                act.dma_start(rows[r:r + n, :], ap).then_inc(S["rows_in"], 16)

            rs(C_BADA, 24, b_ada[0].rearrange("(k p) -> k p", p=P))
            rs(C_NORM, 8, norm_w[0].rearrange("(k p) -> k p", p=P))
            rs(C_BG, 16, b_gate[0].rearrange("(k p) -> k p", p=P))
            rs(C_CB, 4, conv_b[0].rearrange("(k p) -> k p", p=P))
            rs(C_LW, 4, conv_ln_w[0].rearrange("(k p) -> k p", p=P))
            rs(C_LB, 4, conv_ln_b[0].rearrange("(k p) -> k p", p=P))
            for r, ap in ((C_Q, q_norm_w), (C_K, k_norm_w)):
                act.dma_start(rows[r:r + 1, :].rearrange("a (b n) -> a b n", b=2),
                              ap.unsqueeze(1).to_broadcast([1, 2, HD])).then_inc(S["rows_in"], 16)
            act.dma_start(conv_rows[:, :], conv_w[0]).then_inc(S["rows_in"], 16)
            act.dma_start(gate_bc[:, :], b_ada[0:1, 2 * D:3 * D].to_broadcast([P, D])).then_inc(S["gate_bias"], 16)

            act.wait_ge(S["c_col"], 1)
            act.activation(small[:, SC:SC + KB], bank[1][:, 0:KB], ACT.Silu).then_inc(S["sc_ready"], 1)

            def w_high(n):
                act.wait_ge(raw_in[n % RAW], 16 * (n // RAW + 1))
                if n >= WR:
                    if BLOCKS[n - WR][0] == "out":
                        nn, kk = divmod(BLOCKS[n - WR][1], 4)
                        if kk < 3:
                            act.wait_ge(S["out_ready"], 3 * nn + kk + 1)
                        else:
                            act.wait_ge(S["out_full"], NT * (nn + 1))
                    else:
                        act.wait_ge(S["pj_ready"], LAST_SEG[n - WR] + 1)
                act.activation(w_hi[:, n % WR, :], raw[:, n % RAW, :], ACT.Copy).then_inc(S["w_hi_done"], 1)

            def x_stats(i0):
                for i in range(i0, i0 + 4):
                    act.wait_ge(x_in[i // 2], 16)
                    link(act.activation(junk[:, :], xt[:, i, :], ACT.Square, accum_out=small[:, SS + i:SS + i + 1]))
                act.activation(small[:, RS + i0:RS + i0 + 4], small[:, SS + i0:SS + i0 + 4], ACT.Sqrt, bias=eps[:, :],
                               scale=1.0 / D).then_inc(S["xsq"], 1)

            def h_out(tt, ks=range(KB)):
                for k in ks:
                    m = KB * tt + k
                    act.wait_ge(S["xt_ready"], m + 1)
                    if m >= 2:
                        act.wait_ge(S["h_ready"], m - 1)
                    for dst in (h_hi[:, k, tt * HALF:(tt + 1) * HALF], h32[:, m % 2, :])[k % 2:]:
                        ins = act.activation(dst, bank[2 + m % 5][:, :], ACT.Identity,
                                             scale=small[:, SCALE_ + k:SCALE_ + k + 1],
                                             bias=small[:, SHIFT + k:SHIFT + k + 1])
                    ins.then_inc(S["h_copied"], 1)

            def out_of(kind, w, tt, dst, func, **kw):
                s = SEG[(kind, w, tt)]
                act.wait_ge(S["pj_ready"], s + 1)
                return act.activation(dst, proj_bank[s % 2][:, :], func, **kw), pj_free[s % 2]

            def conv_input(kind, cc, tt):
                if kind == "convz":
                    ins, free = out_of("convz", cc, tt, zc[:, cc, tt * HALF:(tt + 1) * HALF], ACT.Silu)
                else:
                    base_, func = (0, ACT.Sigmoid) if kind == "convb" else (2, ACT.Copy)
                    if cc:
                        act.wait_ge(S["glu_ready"], 2 * (cc - 1) + tt + 1)
                    ins, free = out_of(kind, cc, tt, sg[:, base_ + tt, :], func)
                ins.then_inc(free, 1)

            def x_scale(i0):
                act.wait_ge(S["rstd_x"], i0 // 4 + 1)
                for i in range(i0, i0 + 4):
                    act.activation(xt[:, i, :], xt[:, i, :], ACT.Copy,
                                   scale=small[:, SS + i:SS + i + 1]).then_inc(S["x_scaled"], 1)

            x_stats(0)
            x_scale(0)
            act.wait_ge(S["cols_ready"], 1)
            act.activation(cols[:, 0:NROWS], bank[0][:, 0:NROWS], ACT.Copy)
            act.activation(conv_col[:, :, :], bank[0][:, 128:256].rearrange("p (c k) -> p c k", k=32)[:, :, 0:TAPS],
                           ACT.Copy).then_inc(S["cols_copied"], 1)
            w_high(0)
            act.wait_ge(S["mod_ready"], 1)
            h_out(0, range(4))
            w_high(1)
            x_stats(4)
            x_scale(4)
            act.wait_ge(S["mod_ready"], 2)
            h_out(0, range(4, KB))
            conv_input(*conv_halves(0)[0])
            w_high(2)
            conv_input(*conv_halves(0)[1])
            h_out(1)
            act.wait_ge(S["h_ready"], 16)
            def next_weights(kind, w, tt):
                if tt == 0:
                    w_high(NO[(kind, w)] + 2)

            def tap_product(c, i):
                k = TAPS - POOL_TAPS + i
                act.wait_ge(S["glu_ready"], 2 * c + 2)
                t = (POOL_TAPS - 1) * c + i - 1
                if i == 0 and c >= 2:
                    act.wait_ge(S["conv_done"], c - 1)
                if i and t >= 2:
                    act.wait_ge(S["tap_added"], t - 1)
                dst = tap[:, t % 2, :] if i else tap_sum[:, c % 2, :]
                bias = {} if i else {"bias": cols[:, C_CB + c:C_CB + c + 1]}
                act.activation(dst, glu[:, c % 2, k:k + T], ACT.Identity, scale=conv_col[:, c, k:k + 1],
                               **bias).then_inc(S["tap_made"], 1)

            def gate_sigmoid(kind, j, tt, col):
                if kind == "gA" and j >= 2:
                    wait_copied(act, ("yA", j - 2, tt))
                if kind == "gB" and j >= 6:
                    wait_copied(act, ("yB", j - 6, tt))
                ins, free = out_of(kind, j, tt, gate_tile(kind, j, tt), ACT.Sigmoid,
                                   bias=cols[:, C_BG + col + j:C_BG + col + j + 1])
                ins.then_inc(free, 1)
                next_weights(kind, j, tt)

            def conv_high():
                act.wait_ge(S["conv_done"], CB)
                for cc in range(CB):
                    act.activation(c_hi[:, cc, :], cv[:, cc, :], ACT.Copy).then_inc(S["conv_hi"], 1)

            for step, (kind, ch, tt, weights, taps) in enumerate(conv_schedule()):
                if step >= 2:
                    if kind == "gB":
                        if (ch, tt) == (0, 0):
                            act.wait_ge(S["glu_ready"], 2 * CB)
                        if (ch, tt) == (GB_BEFORE - 1, 1):
                            conv_high()
                        gate_sigmoid(kind, ch, tt, KB)
                    else:
                        conv_input(kind, ch, tt)
                        if weights:
                            w_high(weights)
                for tap_ in taps:
                    tap_product(*tap_)

            def ln_squares(tt):
                for cc in range(CB):
                    act.wait_ge(S["centered"], CB * tt + cc + 1)
                    half = slice(tt * HALF, (tt + 1) * HALF)
                    if tt:
                        act.wait_ge(S["sq_ready"], cc + 1)
                    act.activation(square_tile(cc), cv[:, cc, half], ACT.Square)
                    act.activation(c_hi[:, cc, half], cv[:, cc, half], ACT.Square).then_inc(S["ln_sq_hi"], 1)

            def ln_rstd(tt):
                act.wait_ge(S["var_ready"], CB * (tt + 1))
                r = glu[:, 1, tt * HALF:(tt + 1) * HALF]
                act.preload_act_table_set("natural_log_exp_and_others")
                link(act.activation(r, bank[3 + 2 * tt][:, :], ACT.Ln, bias=eps[:, :]))
                act.activation(r, r, ACT.Exp, scale=-0.5).then_inc(S["ln_r"], 1)

            def ln_swish(tt):
                for cc in range(CB):
                    half = cv[:, cc, tt * HALF:(tt + 1) * HALF]
                    act.wait_ge(S["ln_scaled"], CB * tt + cc + 1)
                    act.activation(half, half, ACT.Silu, scale=cols[:, C_LW + cc:C_LW + cc + 1],
                                   bias=cols[:, C_LB + cc:C_LB + cc + 1]).then_inc(S["ln_silu"], 1)

            def c_high(tt):
                for cc in range(CB):
                    half = slice(tt * HALF, (tt + 1) * HALF)
                    act.wait_ge(S["ln_z"], CB * tt + cc + 1)
                    act.activation(c_hi[:, cc, half], cv[:, cc, half], ACT.Copy).then_inc(S["c_hi_done"], 1)

            ln_squares(0)
            ln_squares(1)
            gate_sigmoid("gB", 3, 0, KB)
            ln_rstd(0)
            ln_swish(0)
            gate_sigmoid("gB", 3, 1, KB)
            ln_rstd(1)
            gate_sigmoid("gB", 4, 0, KB)
            ln_swish(1)
            gate_sigmoid("gB", 4, 1, KB)
            c_high(0)
            c_high(1)
            gate_sigmoid("gB", 5, 0, KB)
            gate_sigmoid("gB", 5, 1, KB)

            def send_parts(j0):
                for j in (j0, j0 + 1):
                    for tt in range(2):
                        wait_copied(act, ("yB", j, tt))
                    act.dma_start(part_dram.ap()[j], zc[:, j % 4, :]).then_inc(part_out[j % 4], 16)

            w_high(NO[("pB", 2)])
            w_high(NO[("pB", 2)] + 1)
            send_parts(0)
            w_high(NO[("pB", 2)] + 2)
            send_parts(2)
            for j in (6, 7):
                for tt in range(2):
                    gate_sigmoid("gB", j, tt, KB)
            send_parts(4)
            w_high(NO[("q", 0)] + 1)
            def exps(a, i):
                g = a % GROUPS
                u = NT * a + i
                act.wait_ge(S["smax_done"], u + 1)
                n = 2 * P if has_previous(g, i) else P
                o = out_tile(a)
                for hh in range(2):
                    pr = probs[:, u % 2, hh * 2 * P:hh * 2 * P + n]
                    ins = act.activation(pr, pr, ACT.Exp, bias=negmax[:, u % 2, hh:hh + 1],
                                         accum_out=o[:, i, 2 * HD + 2 + hh:2 * HD + 3 + hh])
                ins.then_inc(S["exp_done"], 1)

            def output(a, i):
                u = NT * a + i
                act.wait_ge(S["o_ready"], u + 1)
                act.activation(out_tile(a)[:, i, 0:2 * HD], o_bank[:, 0:2 * HD], ACT.Copy).then_inc(S["o_out"], 1)
                p, g = divmod(a, GROUPS)
                if g and i == NT - 1:
                    act.wait_ge(S["o_out"], u + 1)
                    o, dram, done = out_tile(a), o_dram[g - 1].ap()[p], S[f"o_sent{g}"]
                    if g == 1:
                        dst = dram.rearrange("(b l r) w -> b l r w", b=2, r=4)
                        for b in range(2):
                            act.dma_start(dst[b], o[:, b::2, :]).then_inc(done, 16)
                    else:
                        dst = dram.rearrange("(l i e) w -> e l i w", i=8, e=2)
                        for e in range(2):
                            act.dma_start(dst[e], o[e * HD:(e + 1) * HD, :, :]).then_inc(done, 16)

            def take_z(tt):
                if tt == 0:
                    act.wait_ge(S["qk_ready"], 4 * STAGES)
                ins, free = out_of("z", 0, tt, qk_raw[:, tt, :], ACT.Copy)
                ins.then_inc(free, 1)

            def take(st, m):
                g = st % GROUPS
                if m < 4:
                    k = 4 * st + m
                    if k >= 2:
                        act.wait_ge(S["qk_ready"], k - 1)
                    ins, free = out_of("qk"[m // 2], st, m % 2, qk_raw[:, m % 2, :], ACT.Copy)
                    ins.then_inc(free, 1)
                    act.wait_ge(free, SEG[("qk"[m // 2], st, m % 2)] // 2 + 1)
                    act.activation(rstd[:, m % 2, :], qk_raw[:, m % 2, :], ACT.Square)
                    act.activation(sq_hi[:, m % 2, :], qk_raw[:, m % 2, :], ACT.Square).then_inc(S["sq_hi_done"], 1)
                else:
                    if st and m == 4:
                        act.wait_ge(S["vtr_ready"], 2 * st)
                    s = SEG[("v", st, m - 4)]
                    act.wait_ge(S["pj_ready"], s + 1)
                    ins = act.activation(token_order(vT[:, :], g, m - 4), natural(proj_bank[s % 2][:, :], g), ACT.Copy)
                    ins.then_inc(pj_free[s % 2], 1)

            def head_rstd(st, m):
                act.wait_ge(S["ss_ready"], 4 * st + m + 1)
                r = rstd[:, m % 2, :]
                act.activation(r, aux[:, :], ACT.Ln, bias=eps[:, :]).then_inc(S["ln_done"], 1)
                act.wait_ge(S["ln_done"], 4 * st + m + 1)
                act.activation(r, r, ACT.Exp, scale=-0.5).then_inc(S["rstd_done"], 1)

            def values(a, hh):
                act.wait_ge(S["vtr_ready"], 2 * a + hh + 1)
                act.activation(v[:, 4 * hh:4 * hh + 4, :], aux[:, :].rearrange("p (i n) -> p i n", i=4),
                               ACT.Copy).then_inc(S["v_ready"], 1)

            def comb_exp(p):
                act.wait_ge(S["comb_d"], p + 1)
                act.activation(cmb[:, 1:4, :, :], cmb[:, 1:4, :, :], ACT.Exp).then_inc(S["comb_e"], 1)

            send_parts(KB - 2)
            for q in part_out:
                act.wait_ge(q, 32)
            act.preload_act_table_set("natural_log_exp_and_others")
            for st in range(STAGES + 1):
                for slot in range(SLOTS):
                    m, k = divmod(slot, 8)
                    if st and slot % 5 == 3 and slot // 5 < NT:
                        exps(st - 1, slot // 5)
                    if k == 2 and m % 2:
                        w_high(NO[("q", 0)] + 3 * st + m // 2 + 2)
                    if k == 0:
                        if m == 0 and st:
                            take(st - 1, 5)
                        if 1 <= m and st < STAGES:
                            take(st, m - 1)
                        if m == 5 and st == STAGES:
                            take_z(0)
                        if 1 <= m <= 4 and st == STAGES:
                            j, tt = divmod(m - 1, 2)
                            ins, free = out_of("gA", j, tt, gate_tile("gA", j, tt), ACT.Identity,
                                               bias=cols[:, C_BG + j:C_BG + j + 1])
                            ins.then_inc(free, 1)
                    if k == 6 and 1 <= m <= 4 and st < STAGES:
                        head_rstd(st, m - 1)
                    if not st:
                        continue
                    a = st - 1
                    if slot == 4:
                        values(a, 0)
                    if slot == 7:
                        values(a, 1)
                    if slot % 5 == 0 and slot // 5 >= 2:
                        output(a, slot // 5 - 2)
                    if slot == 36 and st >= 4 and (st - 4) % 3 == 0:
                        comb_exp((st - 4) // 3)

            for e in range(4):
                tile = sg[:, e, :]
                wait_copied(act, ("gA", e // 2, e % 2))
                act.activation(tile, tile, ACT.Sigmoid).then_inc(S["ga_sigmoid"], 1)
            take_z(1)
            for tt in range(2):
                wait_copied(act, ("z", 0, tt))
                act.activation(z_silu[:, tt, :], qk_raw[:, tt, :], ACT.Silu).then_inc(S["zs_ready"], 1)
            for e in range(8):
                p, tt = divmod(e, 2)
                if e >= 2:
                    act.wait_ge(S["a32_made"], e - 1)
                    ins, free = out_of("z", p, tt, z_silu[:, e % 2, :], ACT.Silu)
                    ins.then_inc(free, 1)
                    next_weights("z", p, tt)
                if e >= 1:
                    a_high(e - 1, act)
                if e == 2:
                    comb_exp(PAIRS - 1)
            a_high(7, act)
            w_high(NO[("pA", 0)] + 2)
            for i in range(1, KB // 2):
                for j in (2 * i, 2 * i + 1):
                    for tt in range(2):
                        gate_sigmoid("gA", j, tt, 0)
                w_high(NO[("pA", i)] + 2)

            def load_x_again(k):
                nn, t = divmod(k, NT)
                if k >= NT:
                    act.wait_ge(out_made[k % 2], (k - NT) // 2 + 1)
                act.dma_start(x_tile(k), x3[:, t, nn * HALF:(nn + 1) * HALF]).then_inc(x_again[k % NT], 16)

            act.wait_ge(S["tr_ready"], 8)
            for k in range(NT):
                load_x_again(k)
            act.wait_ge(S["pj_ready"], SEG[("gA", KB - 1, 1)] + 1)
            for k in range(KB):
                for tt in range(2):
                    act.wait_ge(S["merged_ready"], 2 * k + tt + 1)
                    act.activation(h_hi[:, k, tt * HALF:(tt + 1) * HALF], merged[:, k, tt * HALF:(tt + 1) * HALF],
                                   ACT.Copy).then_inc(S["m_hi_done"], 1)
            for n in range(NO[("out", 2)], NO[("out", 7)]):
                w_high(n)
            w_high(NO[("out", 7)])
            for k in range(NT, 2 * NT):
                load_x_again(k)

        @block.vector
        def _(dve):
            chain = [0]

            def link(ins):
                chain[0] += 1
                ins.then_inc(S["dve_chain"], 1)
                dve.wait_ge(S["dve_chain"], chain[0])

            dve.wait_ge(S["sc_ready"], 1)

            def h_split(m):
                tt, k = divmod(m, KB)
                half = slice(tt * HALF, (tt + 1) * HALF)
                dve.wait_ge(S["h_copied"], m + 1)
                if k % 2:
                    link(dve.tensor_copy(h_hi[:, k, half], h32[:, m % 2, :]))
                dve.tensor_tensor(h_lo[:, k, half], h32[:, m % 2, :], h_hi[:, k, half].bitcast(F32),
                                  ALU.subtract).then_inc(S["h_ready"], 1)

            def ada_sum(n):
                part, k = divmod(n, KB)
                dve.wait_ge(ada_in[n % ADA], 16 * (n // ADA + 1))
                sc = small[:, SC + k:SC + k + 1]
                dst = ada_part[:, part * D:(part + 1) * D]
                if k == 0:
                    ins = dve.tensor_scalar(dst, ada_w[:, n % ADA, :], sc, None, ALU.mult)
                else:
                    dve.wait_ge(S["ada_used"], n)
                    ins = dve.scalar_tensor_tensor(dst, ada_w[:, n % ADA, :], sc, dst, ALU.mult, ALU.add)
                ins.then_inc(S["ada_used"], 1)

            def x_rstd(tt):
                i = 4 * tt
                dve.wait_ge(S["xsq"], tt + 1)
                dve.reciprocal(small[:, SS + i:SS + i + 4], small[:, RS + i:RS + i + 4]).then_inc(S["rstd_x"], 1)

            def modulation(part):
                dve.wait_ge(S["ada_cols"], part + 1)
                dve.wait_ge(S["cols_copied"], 1)
                blk = slice(4 * part, 4 * part + 4)
                mod = [ap.rearrange("p (s k) -> p s k", s=2)[:, :, blk] for ap in
                       (small[:, SHIFT:SHIFT + 16], bank[7][:, 0:16], cols[:, C_BADA:C_BADA + 16])]
                link(dve.tensor_tensor(*mod, ALU.add))
                scale = small[:, SCALE_ + 4 * part:SCALE_ + 4 * part + 4]
                dve.scalar_tensor_tensor(scale, scale, 1.0, cols[:, C_NORM + 4 * part:C_NORM + 4 * part + 4],
                                         ALU.add, ALU.mult).then_inc(S["mod_ready"], 1)

            for n in range(4):
                ada_sum(n)
            x_rstd(0)
            for n in range(4, KB + 1):
                ada_sum(n)
            modulation(0)
            h_split(0)
            h_split(1)
            ada_sum(KB + 1)
            h_split(2)
            ada_sum(KB + 2)
            h_split(3)
            for n in range(KB + 3, 2 * KB):
                ada_sum(n)
                if n == KB + 4:
                    x_rstd(1)
            modulation(1)
            for m in range(4, 2 * KB):
                h_split(m)
            link(dve.tensor_scalar(cols[:, C_Q:C_Q + 1], cols[:, C_Q:C_Q + 1], float(HD) ** -0.5, None, ALU.mult))
            dve_taps = TAPS - POOL_TAPS
            for cc in range(CB):
                dve.wait_ge(S["glu_ready"], 2 * cc + 2)
                sums = [cv[:, cc, :], acc_b[:, :]]
                g_ = glu[:, cc % 2, :]
                for k in range(dve_taps):
                    dst = sums[k % 2]
                    w = conv_col[:, cc, k:k + 1]
                    if k < 2:
                        ins = dve.tensor_scalar(dst, g_[:, k:k + T], w, None, ALU.mult)
                    else:
                        dve.wait_ge(S["conv_part"], (dve_taps + 1) * cc + k - 1)
                        ins = dve.scalar_tensor_tensor(dst, g_[:, k:k + T], w, dst, ALU.mult, ALU.add)
                    ins.then_inc(S["conv_part"], 1)
                dve.wait_ge(S["conv_part"], (dve_taps + 1) * cc + dve_taps)
                dve.tensor_tensor(sums[0], sums[0], sums[1], ALU.add).then_inc(S["conv_part"], 1)
                dve.wait_ge(S["conv_part"], (dve_taps + 1) * (cc + 1))
                dve.wait_ge(S["tap_added"], (POOL_TAPS - 1) * (cc + 1))
                dve.tensor_tensor(sums[0], sums[0], tap_sum[:, cc % 2, :], ALU.add).then_inc(S["conv_done"], 1)

            for cc in range(CB):
                dve.wait_ge(S["conv_hi"], cc + 1)
                dve.tensor_tensor(c_lo[:, cc, :], cv[:, cc, :], c_hi[:, cc, :].bitcast(F32),
                                  ALU.subtract).then_inc(S["conv_lo"], 1)
            for tt in range(2):
                dve.wait_ge(S["mean_ready"], tt + 1)
                for cc in range(CB):
                    half = cv[:, cc, tt * HALF:(tt + 1) * HALF]
                    dve.tensor_tensor(half, half, bank[2 + 2 * tt][:, :], ALU.subtract).then_inc(S["centered"], 1)
            for tt in range(2):
                half = slice(tt * HALF, (tt + 1) * HALF)
                for cc in range(CB):
                    dve.wait_ge(S["ln_sq_hi"], CB * tt + cc + 1)
                    dve.tensor_tensor(c_lo[:, cc, half], square_tile(cc), c_hi[:, cc, half].bitcast(F32),
                                      ALU.subtract).then_inc(S["sq_ready"], 1)
            for tt in range(2):
                dve.wait_ge(S["ln_r"], tt + 1)
                for cc in range(CB):
                    half = cv[:, cc, tt * HALF:(tt + 1) * HALF]
                    dve.tensor_tensor(half, half, glu[:, 1, tt * HALF:(tt + 1) * HALF],
                                      ALU.mult).then_inc(S["ln_scaled"], 1)
            for tt in range(2):
                half = slice(tt * HALF, (tt + 1) * HALF)
                for cc in range(CB):
                    dve.wait_ge(S["ln_silu"], CB * tt + cc + 1)
                    dve.tensor_tensor(cv[:, cc, half], cv[:, cc, half], zc[:, cc, half],
                                      ALU.mult).then_inc(S["ln_z"], 1)
                for cc in range(CB):
                    dve.wait_ge(S["c_hi_done"], CB * tt + cc + 1)
                    dve.tensor_tensor(c_lo[:, cc, half], cv[:, cc, half], c_hi[:, cc, half].bitcast(F32),
                                      ALU.subtract).then_inc(S["c_ready"], 1)
            for j in range(KB):
                for tt in range(2):
                    s = SEG[("yB", j, tt)]
                    k = 2 * j + tt
                    dve.wait_ge(S["pj_ready"], s + 1)
                    if k == 0:
                        dve.wait_ge(S["ln_z"], 2 * CB)
                    if k >= 8:
                        dve.wait_ge(part_out[j % 4], 16)
                    dst = zc[:, (k % 8) // 2, (k % 2) * HALF:(k % 2 + 1) * HALF]
                    ins = dve.tensor_tensor(dst, gate_tile("gB", j, tt), proj_bank[s % 2][:, :], ALU.mult)
                    ins.then_inc(pj_free[s % 2], 1)

            def maxima(a, i):
                p, g = divmod(a, GROUPS)
                u = NT * a + i
                dve.wait_ge(S["s_ready"], u + 1)
                if u >= 2:
                    dve.wait_ge(S["pt_ready"], u - 1)
                if i == 0 and g == 0 and p >= 2:
                    dve.wait_ge(S["comb_done"], p - 1)
                if i == 0 and g and p:
                    dve.wait_ge(S[f"o_sent{g}"], 32 * p)
                o = out_tile(a)
                mk = mask2[:, :] if g == 2 else mask[:, :] if has_previous(g, i) else mask[:, P:2 * P]
                n = 2 * P if has_previous(g, i) else P
                for hh in range(2):
                    ins = dve.tensor_tensor_reduce(out=probs[:, u % 2, hh * 2 * P:hh * 2 * P + n],
                                                   in0=s_bank[hh][:, 0:n], in1=mk,
                                                   scale=1.0, scalar=-3e38, op0=ALU.add, op1=ALU.max,
                                                   accum_out=o[:, i, 2 * HD + hh:2 * HD + hh + 1])
                link(ins)
                dve.tensor_scalar(negmax[:, u % 2, :], o[:, i, 2 * HD:2 * HD + 2], -1.0, None,
                                  ALU.mult).then_inc(S["smax_done"], 1)

            def transposed(a, i):
                g = a % GROUPS
                u = NT * a + i
                dve.wait_ge(S["pt_ready"], u + 1)
                if u >= 2:
                    dve.wait_ge(S["o_ready"], u - 1)
                n = (4 if has_previous(g, i) else 2) * P
                dve.tensor_copy(pT[:, u % 2, 0:n], pt_bank[u % 2][:, 0:n]).then_inc(S["pt_out"], 1)

            def normalise(st, m):
                g = st % GROUPS
                dve.wait_ge(S["rstd_done"], 4 * st + m + 1)
                if st >= 2 and m == 0:
                    dve.wait_ge(S["s_ready"], NT * (st - 1))
                dst = (qT, kT)[m // 2][:, st % 2, :]
                col = (C_Q, C_K)[m // 2]
                dve.scalar_tensor_tensor(token_order(dst, g, m % 2), natural(qk_raw[:, m % 2, :], g),
                                         cols[:, col:col + 1], natural(rstd[:, m % 2, :], g),
                                         ALU.mult, ALU.mult).then_inc(S["qk_ready"], 1)

            def comb_small(p, part):
                ts = [o_own[p % 2], o_nat[0], o_nat[1]]
                mx = [t[:, :, 2 * HD:2 * HD + 2] for t in ts]
                dn = [t[:, :, 2 * HD + 2:2 * HD + 4] for t in ts]
                e = [cmb[:, 1 + g, :, :] for g in range(3)]
                top = cmb[:, 0, :, :]
                if part == 0:
                    dve.wait_ge(S["nat_in"], 32 * (p + 1))
                    if p:
                        dve.wait_ge(S["comb_done"], p)
                    dve.wait_ge(S["exp_done"], NT * (3 * p + 1))
                    link(dve.tensor_tensor(top, mx[0], mx[1], ALU.max))
                    link(dve.tensor_tensor(top, top, mx[2], ALU.max))
                    for g in range(3):
                        ins = dve.tensor_tensor(e[g], mx[g], top, ALU.subtract)
                    ins.then_inc(S["comb_d"], 1)
                else:
                    dve.wait_ge(S["comb_e"], p + 1)
                    t = cmb[:, 4, :, :]
                    link(dve.tensor_tensor(top, e[0], dn[0], ALU.mult))
                    for g in (1, 2):
                        link(dve.tensor_tensor(t, e[g], dn[g], ALU.mult))
                        link(dve.tensor_tensor(top, top, t, ALU.add))
                    link(dve.reciprocal(t, top))
                    for g in range(3):
                        ins = dve.tensor_tensor(e[g], e[g], t, ALU.mult)
                    ins.then_inc(S["comb_w"], 1)

            def gate_sum(k):
                dve.wait_ge(gate_in[k % 3], 16 * (k // 3 + 1))
                sc = small[:, SC + k:SC + k + 1]
                if k == 0:
                    ins = dve.tensor_scalar(gate_part, gate_w[:, 0, :], sc, None, ALU.mult)
                else:
                    dve.wait_ge(S["ada_used"], 2 * KB + k)
                    ins = dve.scalar_tensor_tensor(gate_part, gate_w[:, k % 3, :], sc, gate_part, ALU.mult, ALU.add)
                ins.then_inc(S["ada_used"], 1)

            for st in range(STAGES + 1):
                for slot in range(SLOTS):
                    m, k = divmod(slot, 8)
                    if k == 1 and 2 <= m <= 5 and st < STAGES:
                        normalise(st, m - 2)
                    if st == 0 and slot % 5 == 2 and slot // 5 < KB:
                        gate_sum(slot // 5)
                    if st == 1 and slot == 0:
                        dve.wait_ge(S["gate_bias"], 16)
                        for hh in range(2):
                            dve.wait_ge(S["gate_mm"], hh + 1)
                            gb = gate_bc[:, hh * HALF:(hh + 1) * HALF]
                            dve.tensor_tensor(gb, pt_bank[hh][:, :], gb, ALU.add).then_inc(S["gate_ready"], 1)
                    if not st:
                        continue
                    a = st - 1
                    i = slot // 5
                    if slot % 5 == 1 and i < NT:
                        maxima(a, i)
                    if slot % 5 == 2 and 1 <= i <= NT:
                        transposed(a, i - 1)
                    if st >= 4 and (st - 4) % 3 == 0:
                        if slot == 34:
                            comb_small((st - 4) // 3, 0)
                        if slot == 40:
                            comb_small((st - 4) // 3, 1)

            for e in range(8):
                p, tt = divmod(e, 2)
                half = slice(tt * HALF, (tt + 1) * HALF)
                if e == 2:
                    comb_small(PAIRS - 1, 0)
                    comb_small(PAIRS - 1, 1)
                dve.wait_ge(S["tr_ready"], e + 1)
                if e < 2:
                    dve.wait_ge(S["zs_ready"], e + 1)
                else:
                    wait_copied(dve, ("z", p, tt))
                if e >= 2:
                    dve.wait_ge(S["a_ready"], e - 1)
                dve.tensor_tensor(a32[:, e % 2, :], bank[2 + e % 2][:, :], z_silu[:, e % 2, :],
                                  ALU.mult).then_inc(S["a32_made"], 1)
                dve.wait_ge(S["a_hi_done"], e + 1)
                dve.tensor_tensor(a_lo[:, p, half], a32[:, e % 2, :], a_hi[:, p, half].bitcast(F32),
                                  ALU.subtract).then_inc(S["a_ready"], 1)
            def merged_low(k):
                half = slice((k % 2) * HALF, (k % 2 + 1) * HALF)
                dve.wait_ge(S["m_hi_done"], k + 1)
                dve.tensor_tensor(h_lo[:, k // 2, half], merged[:, k // 2, half], h_hi[:, k // 2, half].bitcast(F32),
                                  ALU.subtract).then_inc(S["m_ready"], 1)

            for j in range(KB):
                for tt in range(2):
                    s = SEG[("yA", j, tt)]
                    k = 2 * j + tt
                    half = slice(tt * HALF, (tt + 1) * HALF)
                    dve.wait_ge(S["pj_ready"], s + 1)
                    if k == 0:
                        dve.wait_ge(S["a_ready"], 8)
                        dve.wait_ge(S["ga_sigmoid"], 4)
                    dst = y32[:, k % 2, :]
                    ins = dve.tensor_tensor(dst, gate_tile("gA", j, tt), proj_bank[s % 2][:, :], ALU.mult)
                    ins.then_inc(pj_free[s % 2], 1)
                    wait_copied(dve, ("yA", j, tt))
                    dve.wait_ge(part_back[j], 16)
                    dve.tensor_tensor(merged[:, j, half], dst, merged[:, j, half], ALU.add).then_inc(S["merged_ready"], 1)
                    if j >= KB - 2:
                        for i in range(3):
                            merged_low(3 * (k - 12) + i)
            for k in range(12, 16):
                merged_low(k)
            for k in range(16):
                nn, t = divmod(k, NT)
                dve.wait_ge(S["out_full"], k + 1)
                if k >= NT:
                    dve.wait_ge(stored[k % NT], 16)
                dve.tensor_tensor(y_tile(k), bank[t][:, :], gate_bc[:, nn * HALF:(nn + 1) * HALF],
                                  ALU.mult).then_inc(S["out_scaled"], 1)
                if k >= NT and k % 2:
                    dve.wait_ge(S["out_scaled"], k + 1)
                    dve.wait_ge(x_again[k % NT], 16 * (k // NT + 1))
                    dve.tensor_tensor(y_tile(k), y_tile(k), x_tile(k), ALU.add).then_inc(out_made[1], 1)


_INS = ["x", "c", "w_ada", "b_ada", "norm_w", "w_in", "b_gate", "q_norm_w", "k_norm_w", "w_attn_proj",
        "conv_w", "conv_b", "conv_ln_w", "conv_ln_b", "w_conv_proj", "w_out"]


def kernel(**inputs):
    import numpy as _np
    import concourse.bacc as _bacc
    from concourse import mybir as _mybir
    from concourse.bass_utils import run_bass_kernel_spmd as _run

    nc = _bacc.Bacc("TRN2", target_bir_lowering=False, num_devices=1)
    arrays, args = {}, {}
    for name in _INS:
        a = _np.ascontiguousarray(inputs[name])
        arrays[f"in_{name}_dram"] = a
        args[name] = nc.dram_tensor(f"in_{name}_dram", a.shape, _mybir.dt.from_np(a.dtype), kind="ExternalInput").ap()
    args["out"] = nc.dram_tensor("out_0_dram", (1, 1024, 1024), _mybir.dt.float32, kind="ExternalOutput").ap()
    build(nc, **args)
    r = _run(nc, [arrays], core_ids=[0])
    return r.results[0]["out_0_dram"]
```
